# Optimizing a Trainium2 kernel written in Bass

```python
import math
import jax, jax.numpy as jnp
from jax import lax
import numpy as np

D_MODEL = 1024
BATCH = 1
SEQ = 512
DEPTH = 2

GRID_W = 64
CTX_LEN = 256
HEAD_DIM = 64
N_HEADS_TOTAL = D_MODEL // HEAD_DIM
A_HEADS = N_HEADS_TOTAL // 2
A_KV_HEADS = A_HEADS // 4
A_REP = A_HEADS // A_KV_HEADS
B_HEADS = N_HEADS_TOTAL // 4
C_HEADS = N_HEADS_TOTAL // 4
DIFF_DIM = HEAD_DIM // 2
WIN_H_MAX = 8
WIN_W = 16
Q_BLOCK = 128
FFN_DIM = ((8 * D_MODEL // 3 + 127) // 128) * 128
ROPE_THETA = 10000.0
EPS = 1e-6
IN_SIZES = (A_HEADS * HEAD_DIM, A_KV_HEADS * HEAD_DIM, A_KV_HEADS * HEAD_DIM,
            B_HEADS * HEAD_DIM, B_HEADS * HEAD_DIM, B_HEADS * HEAD_DIM,
            C_HEADS * HEAD_DIM, C_HEADS * HEAD_DIM, C_HEADS * HEAD_DIM)
IN_COLS = A_HEADS * HEAD_DIM + 2 * A_KV_HEADS * HEAD_DIM + 3 * B_HEADS * HEAD_DIM + 3 * C_HEADS * HEAD_DIM


def rms_norm(x, g):
    xf = x.astype(jnp.float32)
    y = xf * lax.rsqrt(jnp.mean(xf * xf, axis=-1, keepdims=True) + EPS)
    return y.astype(x.dtype) * g

def modulate(h, shift, scale):
    return h * (1.0 + scale) + shift

def heads(t, n):
    b, s, _ = t.shape
    return t.reshape(b, s, n, -1).transpose(0, 2, 1, 3)

def diff_heads(t):
    b, s, _ = t.shape
    return t.reshape(b, s, C_HEADS, 2, DIFF_DIM).transpose(0, 2, 3, 1, 4)

def merge_heads(o):
    b, h, s, d = o.shape
    return o.transpose(0, 2, 1, 3).reshape(b, s, h * d)

def axial_rope_angles(L, dim):
    half = dim // 2
    inv = ROPE_THETA ** (-jnp.arange(0, half, 2, dtype=jnp.float32) / half)
    t = jnp.arange(L, dtype=jnp.int32)
    row = (t // GRID_W).astype(jnp.float32)
    col = (t % GRID_W).astype(jnp.float32)
    ang = jnp.concatenate([row[:, None] * inv, col[:, None] * inv], axis=-1)
    return jnp.cos(ang), jnp.sin(ang)

def apply_rope(x, cos, sin):
    x1, x2 = x[..., 0::2], x[..., 1::2]
    c = cos.astype(x.dtype)
    s = sin.astype(x.dtype)
    return jnp.stack([x1 * c - x2 * s, x1 * s + x2 * c], axis=-1).reshape(x.shape)

def sweep_blocks(fn, q, axis, out_axis):
    s = q.shape[axis]
    n = s // Q_BLOCK
    qb = jnp.moveaxis(q.reshape(q.shape[:axis] + (n, Q_BLOCK) + q.shape[axis + 1:]), axis, 0)
    o = jnp.moveaxis(lax.map(fn, qb), 0, out_axis)
    return o.reshape(o.shape[:out_axis] + (s,) + o.shape[out_axis + 2:])

def softmax_attend(q, kvs, s_spec, o_spec, scale):
    s = jnp.concatenate([jnp.einsum(s_spec, q, k, preferred_element_type=jnp.float32) for k, _ in kvs], axis=-1) * scale
    p = jax.nn.softmax(s, axis=-1)
    bounds = np.cumsum([k.shape[-2] for k, _ in kvs])[:-1].tolist()
    parts = jnp.split(p, bounds, axis=-1)
    terms = [jnp.einsum(o_spec, pi.astype(v.dtype), v) for pi, (_, v) in zip(parts, kvs)]
    return sum(terms[1:], terms[0])

def diff_attend(q, kvs, lam, scale):
    s = jnp.concatenate([jnp.einsum('bhmqd,bhmkd->bhmqk', q, k, preferred_element_type=jnp.float32)
                         for k, _ in kvs], axis=-1) * scale
    p = jax.nn.softmax(s, axis=-1)
    w = p[:, :, 0] - lam * p[:, :, 1]
    bounds = np.cumsum([k.shape[-2] for k, _ in kvs])[:-1].tolist()
    parts = jnp.split(w, bounds, axis=-1)
    terms = [jnp.einsum('bhqk,bhkd->bhqd', wi.astype(v.dtype), v) for wi, (_, v) in zip(parts, kvs)]
    return sum(terms[1:], terms[0])

def neighbourhood_attend(q, k, v, k_ctx, v_ctx, rpb):
    b, h, L, d = q.shape
    rows = L // GRID_W
    win_h = min(WIN_H_MAX, rows)
    n_win = win_h * WIN_W
    scale = d ** -0.5
    qg = q.reshape(b, h, rows, GRID_W, d)
    kg = k.reshape(b, h, rows, GRID_W, d)
    vg = v.reshape(b, h, rows, GRID_W, d)
    col = jnp.arange(GRID_W)
    col_idx = jnp.clip(col - WIN_W // 2, 0, GRID_W - WIN_W)[:, None] + jnp.arange(WIN_W)[None, :]
    col_bias = rpb[:, :, col_idx - col[:, None] + WIN_W - 1]

    def one_row(r):
        rs = jnp.clip(r - win_h // 2, 0, rows - win_h)
        q_r = lax.dynamic_index_in_dim(qg, r, axis=2, keepdims=False)
        k_win = lax.dynamic_slice_in_dim(kg, rs, win_h, axis=2)[:, :, :, col_idx]
        v_win = lax.dynamic_slice_in_dim(vg, rs, win_h, axis=2)[:, :, :, col_idx]
        row_off = rs + jnp.arange(win_h) - r
        bias = col_bias[:, row_off + WIN_H_MAX - 1].transpose(0, 2, 1, 3)
        s_win = jnp.einsum('bhqd,bhiqjd->bhqij', q_r, k_win, preferred_element_type=jnp.float32) * scale + bias
        s_ctx = jnp.einsum('bhqd,bhkd->bhqk', q_r, k_ctx, preferred_element_type=jnp.float32) * scale
        p = jax.nn.softmax(jnp.concatenate([s_win.reshape(b, h, GRID_W, n_win), s_ctx], axis=-1), axis=-1)
        p_win = p[..., :n_win].reshape(b, h, GRID_W, win_h, WIN_W).astype(v.dtype)
        p_ctx = p[..., n_win:].astype(v.dtype)
        return (jnp.einsum('bhqij,bhiqjd->bhqd', p_win, v_win)
                + jnp.einsum('bhqk,bhkd->bhqd', p_ctx, v_ctx))

    o = lax.map(one_row, jnp.arange(rows))
    return o.transpose(1, 2, 0, 3, 4).reshape(b, h, L, d)

def mixer_a(q, k, v, q_ctx, k_ctx, v_ctx, gq, gk, cos, sin, with_ctx):
    q = apply_rope(rms_norm(heads(q, A_HEADS), gq), cos, sin)
    k = apply_rope(rms_norm(heads(k, A_KV_HEADS), gk), cos, sin)
    v = heads(v, A_KV_HEADS)
    k_ctx = rms_norm(heads(k_ctx, A_KV_HEADS), gk)
    v_ctx = heads(v_ctx, A_KV_HEADS)
    b, _, L, d = q.shape
    scale = d ** -0.5
    s_spec, o_spec = 'bgrqd,bgkd->bgrqk', 'bgrqk,bgkd->bgrqd'
    qg = q.reshape(b, A_KV_HEADS, A_REP, L, d)
    o = sweep_blocks(lambda qb: softmax_attend(qb, ((k, v), (k_ctx, v_ctx)), s_spec, o_spec, scale), qg, 3, 3)
    out = merge_heads(o.reshape(b, A_HEADS, L, d))
    out_ctx = None
    if with_ctx:
        qc = rms_norm(heads(q_ctx, A_HEADS), gq)
        lc = qc.shape[2]
        oc = softmax_attend(qc.reshape(b, A_KV_HEADS, A_REP, lc, d), ((k_ctx, v_ctx),), s_spec, o_spec, scale)
        out_ctx = merge_heads(oc.reshape(b, A_HEADS, lc, d))
    return out, out_ctx

def mixer_b(q, k, v, q_ctx, k_ctx, v_ctx, gq, gk, rpb, with_ctx):
    q = rms_norm(heads(q, B_HEADS), gq)
    k = rms_norm(heads(k, B_HEADS), gk)
    v = heads(v, B_HEADS)
    k_ctx = rms_norm(heads(k_ctx, B_HEADS), gk)
    v_ctx = heads(v_ctx, B_HEADS)
    out = merge_heads(neighbourhood_attend(q, k, v, k_ctx, v_ctx, rpb))
    out_ctx = None
    if with_ctx:
        qc = rms_norm(heads(q_ctx, B_HEADS), gq)
        oc = softmax_attend(qc, ((k_ctx, v_ctx),), 'bhqd,bhkd->bhqk', 'bhqk,bhkd->bhqd', HEAD_DIM ** -0.5)
        out_ctx = merge_heads(oc)
    return out, out_ctx

def mixer_c(q, k, v, q_ctx, k_ctx, v_ctx, gq, gk, lq1, lk1, lq2, lk2, g_sub, lam_init, cos, sin, with_ctx):
    lam = (jnp.exp(jnp.sum(lq1.astype(jnp.float32) * lk1.astype(jnp.float32)))
           - jnp.exp(jnp.sum(lq2.astype(jnp.float32) * lk2.astype(jnp.float32))) + lam_init)
    q = apply_rope(rms_norm(diff_heads(q), gq), cos, sin)
    k = apply_rope(rms_norm(diff_heads(k), gk), cos, sin)
    v = heads(v, C_HEADS)
    k_ctx = rms_norm(diff_heads(k_ctx), gk)
    v_ctx = heads(v_ctx, C_HEADS)
    scale = DIFF_DIM ** -0.5
    o = sweep_blocks(lambda qb: diff_attend(qb, ((k, v), (k_ctx, v_ctx)), lam, scale), q, 3, 2)
    out = merge_heads(rms_norm(o, g_sub) * (1.0 - lam_init))
    out_ctx = None
    if with_ctx:
        qc = rms_norm(diff_heads(q_ctx), gq)
        oc = diff_attend(qc, ((k_ctx, v_ctx),), lam, scale)
        out_ctx = merge_heads(rms_norm(oc, g_sub) * (1.0 - lam_init))
    return out, out_ctx

def dwconv3(x, w, b):
    xp = jnp.pad(x, ((0, 0), (1, 1), (0, 0)))
    return xp[:, :-2] * w[0] + xp[:, 1:-1] * w[1] + xp[:, 2:] * w[2] + b

def conv_ffn(h, w_up, conv_w, conv_b, w_down):
    ug = dwconv3(h @ w_up, conv_w, conv_b)
    u, g = jnp.split(ug, 2, axis=-1)
    return (jax.nn.silu(g) * u) @ w_down

def first_inputs(seed: int = 0) -> dict:
    key = jax.random.key(seed)
    ks = jax.random.split(key, 26)
    D = D_MODEL

    def nrm(k, shape, s):
        return jax.random.normal(k, shape, jnp.float32) * s

    return {
        "x": nrm(ks[0], (BATCH, SEQ, D), 1.0),
        "c": nrm(ks[1], (BATCH, D), 1.0),
        "ctx": nrm(ks[2], (BATCH, CTX_LEN, D), 1.0),
        "c_ctx": nrm(ks[3], (D,), 1.0),
        "w_ada": nrm(ks[4], (DEPTH, D, 6 * D), 0.5 * D ** -0.5),
        "b_ada": nrm(ks[5], (DEPTH, 6 * D), 0.01),
        "g_norm1": 1.0 + nrm(ks[6], (DEPTH, D), 0.01),
        "w_in": nrm(ks[7], (DEPTH, D, IN_COLS), D ** -0.5),
        "gq_a": 1.0 + nrm(ks[8], (DEPTH, HEAD_DIM), 0.01),
        "gk_a": 1.0 + nrm(ks[9], (DEPTH, HEAD_DIM), 0.01),
        "gq_b": 1.0 + nrm(ks[10], (DEPTH, HEAD_DIM), 0.01),
        "gk_b": 1.0 + nrm(ks[11], (DEPTH, HEAD_DIM), 0.01),
        "rpb_b": nrm(ks[12], (DEPTH, B_HEADS, 2 * WIN_H_MAX - 1, 2 * WIN_W - 1), 0.02),
        "gq_c": 1.0 + nrm(ks[13], (DEPTH, DIFF_DIM), 0.01),
        "gk_c": 1.0 + nrm(ks[14], (DEPTH, DIFF_DIM), 0.01),
        "lambda_q1": nrm(ks[15], (DEPTH, DIFF_DIM), 0.1),
        "lambda_k1": nrm(ks[16], (DEPTH, DIFF_DIM), 0.1),
        "lambda_q2": nrm(ks[17], (DEPTH, DIFF_DIM), 0.1),
        "lambda_k2": nrm(ks[18], (DEPTH, DIFF_DIM), 0.1),
        "g_subln": 1.0 + nrm(ks[19], (DEPTH, 2 * DIFF_DIM), 0.01),
        "w_out": nrm(ks[20], (DEPTH, D, D), D ** -0.5),
        "g_norm2": 1.0 + nrm(ks[21], (DEPTH, D), 0.01),
        "w_up": nrm(ks[22], (DEPTH, D, 2 * FFN_DIM), D ** -0.5),
        "conv_w": nrm(ks[23], (DEPTH, 3, 2 * FFN_DIM), 3 ** -0.5),
        "conv_b": nrm(ks[24], (DEPTH, 2 * FFN_DIM), 0.01),
        "w_down": nrm(ks[25], (DEPTH, FFN_DIM, D), FFN_DIM ** -0.5),
    }

def first_block(x, c, ctx, c_ctx, w_ada, b_ada, g_norm1, w_in, gq_a, gk_a, gq_b, gk_b, rpb_b, gq_c, gk_c,
              lambda_q1, lambda_k1, lambda_q2, lambda_k2, g_subln, w_out, g_norm2, w_up, conv_w, conv_b, w_down):
    L = x.shape[1]
    cos_a, sin_a = axial_rope_angles(L, HEAD_DIM)
    cos_c, sin_c = axial_rope_angles(L, DIFF_DIM)
    silu_c = jax.nn.silu(c)
    silu_cc = jax.nn.silu(c_ctx)
    bounds = np.cumsum(IN_SIZES)[:-1].tolist()
    for l in range(DEPTH):
        with_ctx = l < DEPTH - 1
        lam_init = 0.8 - 0.6 * math.exp(-0.3 * l)
        mod_x = (silu_c @ w_ada[l] + b_ada[l])[:, None, :]
        mod_c = (silu_cc @ w_ada[l] + b_ada[l])[None, None, :]
        sh1_x, sc1_x, gt1_x, sh2_x, sc2_x, gt2_x = jnp.split(mod_x, 6, axis=-1)
        sh1_c, sc1_c, gt1_c, sh2_c, sc2_c, gt2_c = jnp.split(mod_c, 6, axis=-1)

        hx = modulate(rms_norm(x, g_norm1[l]), sh1_x, sc1_x)
        hc = modulate(rms_norm(ctx, g_norm1[l]), sh1_c, sc1_c)
        qa, ka, va, qb, kb, vb, qc, kc, vc = jnp.split(hx @ w_in[l], bounds, axis=-1)
        qa_t, ka_t, va_t, qb_t, kb_t, vb_t, qc_t, kc_t, vc_t = jnp.split(hc @ w_in[l], bounds, axis=-1)

        oa, oa_t = mixer_a(qa, ka, va, qa_t, ka_t, va_t, gq_a[l], gk_a[l], cos_a, sin_a, with_ctx)
        ob, ob_t = mixer_b(qb, kb, vb, qb_t, kb_t, vb_t, gq_b[l], gk_b[l], rpb_b[l], with_ctx)
        oc, oc_t = mixer_c(qc, kc, vc, qc_t, kc_t, vc_t, gq_c[l], gk_c[l], lambda_q1[l], lambda_k1[l],
                           lambda_q2[l], lambda_k2[l], g_subln[l], lam_init, cos_c, sin_c, with_ctx)

        x = x + gt1_x * (jnp.concatenate([oa, ob, oc], axis=-1) @ w_out[l])
        hx2 = modulate(rms_norm(x, g_norm2[l]), sh2_x, sc2_x)
        x = x + gt2_x * conv_ffn(hx2, w_up[l], conv_w[l], conv_b[l], w_down[l])

        if with_ctx:
            ctx = ctx + gt1_c * (jnp.concatenate([oa_t, ob_t, oc_t], axis=-1) @ w_out[l])
            hc2 = modulate(rms_norm(ctx, g_norm2[l]), sh2_c, sc2_c)
            ctx = ctx + gt2_c * conv_ffn(hc2, w_up[l], conv_w[l], conv_b[l], w_down[l])
    return x


CHUNK = 64
QBLOCK = 128
MIX_WIDTH = D_MODEL
CONV_WIDTH = MIX_WIDTH // 4
CONV_K = 3
ATT_WIDTH = (MIX_WIDTH - CONV_WIDTH) // 2
DSA_HEADS = ATT_WIDTH // HEAD_DIM
CHK_HEADS = ATT_WIDTH // HEAD_DIM
ROPE_DIM = HEAD_DIM // 4
ROPE_THETA_2 = 500000.0
IDX_HEADS = 8
IDX_DIM = 32
IDX_ROPE_DIM = IDX_DIM // 4
TOPK_MAX = 256
BAND_CHUNKS = 8
REL_CLIP = 128
REL_SIZE = (CHUNK - 1) + REL_CLIP + 1
MEM_LEN = 256
MEM_HEADS = 4
MEM_HEAD_DIM = D_MODEL // MEM_HEADS
D_FF = 4 * D_MODEL
LN_EPS = 1e-5
ALPHA = (2.0 * DEPTH) ** 0.25
BETA = (8.0 * DEPTH) ** -0.25
IN_SIZES_2 = (CONV_WIDTH, CONV_WIDTH, CONV_WIDTH,
            DSA_HEADS * HEAD_DIM, HEAD_DIM, HEAD_DIM,
            IDX_HEADS * IDX_DIM, IDX_DIM, IDX_HEADS,
            CHK_HEADS * HEAD_DIM, CHK_HEADS * HEAD_DIM, CHK_HEADS * HEAD_DIM)
IN_WIDTH = sum(IN_SIZES_2)


def layer_norm(x, g, b):
    xf = x.astype(jnp.float32)
    mu = jnp.mean(xf, axis=-1, keepdims=True)
    var = jnp.mean(jnp.square(xf - mu), axis=-1, keepdims=True)
    y = (xf - mu) * lax.rsqrt(var + LN_EPS) * g.astype(jnp.float32) + b.astype(jnp.float32)
    return y.astype(x.dtype)

def partial_rope(x, positions, rot_dim):
    half = rot_dim // 2
    inv_freq = jnp.power(jnp.float32(ROPE_THETA_2), -jnp.arange(half, dtype=jnp.float32) / half)
    ang = positions.astype(jnp.float32)[..., None] * inv_freq
    cos = jnp.cos(ang)[:, :, None, :]
    sin = jnp.sin(ang)[:, :, None, :]
    x1 = x[..., :half].astype(jnp.float32)
    x2 = x[..., half:rot_dim].astype(jnp.float32)
    rot = jnp.concatenate([x1 * cos - x2 * sin, x2 * cos + x1 * sin], axis=-1)
    return jnp.concatenate([rot.astype(x.dtype), x[..., rot_dim:]], axis=-1)

def short_conv_mixer(gate_b, gate_c, h, conv_w):
    u = gate_c * h
    S = u.shape[1]
    u_pad = jnp.pad(u, ((0, 0), (CONV_K - 1, 0), (0, 0)))
    y = conv_w[0] * u_pad[:, 0:S]
    for j in range(1, CONV_K):
        y = y + conv_w[j] * u_pad[:, j:j + S]
    return gate_b * y

def dsa_attention(q, k, v, iq, ik, iw):
    B_, S, H, Dh = q.shape
    nb = S // QBLOCK
    topk = min(TOPK_MAX, S // 4)
    scale = Dh ** -0.5
    key_chunk = jnp.arange(S) // CHUNK
    iw = iw * (IDX_HEADS ** -0.5)

    def to_blocks(a):
        return jnp.moveaxis(a.reshape((B_, nb, QBLOCK) + a.shape[2:]), 1, 0)

    def one_block(args):
        bi, qb, iqb, iwb = args
        q_chunk = (bi * QBLOCK + jnp.arange(QBLOCK)) // CHUNK
        logits = jnp.einsum('bqhd,bsd->bqhs', iqb, ik)
        score = jnp.einsum('bqh,bqhs->bqs', iwb, jax.nn.relu(logits)).astype(jnp.float32)
        admissible = key_chunk[None, :] <= q_chunk[:, None]
        score = jnp.where(admissible[None], score, -jnp.inf)
        _, idx = lax.top_k(score, topk)
        valid = (idx // CHUNK) <= q_chunk[None, :, None]
        k_sel = jax.vmap(lambda a, ii: a[ii])(k, idx)
        v_sel = jax.vmap(lambda a, ii: a[ii])(v, idx)
        s = jnp.einsum('bqhd,bqkd->bhqk', qb, k_sel).astype(jnp.float32) * scale
        s = jnp.where(valid[:, None], s, -jnp.inf)
        p = jax.nn.softmax(s, axis=-1)
        return jnp.einsum('bhqk,bqkd->bqhd', p.astype(v_sel.dtype), v_sel)

    out = lax.map(one_block, (jnp.arange(nb), to_blocks(q), to_blocks(iq), to_blocks(iw)))
    return jnp.moveaxis(out, 0, 1).reshape(B_, S, H * Dh)

def chunk_band_attention(q, k, v, rel_bias):
    B_, S, H, Dh = q.shape
    nc = S // CHUNK
    band = (BAND_CHUNKS + 1) * CHUNK
    pad = BAND_CHUNKS * CHUNK
    scale = Dh ** -0.5
    k_pad = jnp.pad(k, ((0, 0), (pad, 0), (0, 0), (0, 0)))
    v_pad = jnp.pad(v, ((0, 0), (pad, 0), (0, 0), (0, 0)))
    i = jnp.arange(CHUNK)[:, None]
    j = jnp.arange(band)[None, :]
    rel = i - j + pad
    rel_idx = jnp.clip(rel, -(CHUNK - 1), REL_CLIP) + (CHUNK - 1)
    bias = rel_bias[:, rel_idx].astype(jnp.float32)
    q_chunks = jnp.moveaxis(q.reshape(B_, nc, CHUNK, H, Dh), 1, 0)

    def one_chunk(args):
        c, qc = args
        start = c * CHUNK
        kc = lax.dynamic_slice_in_dim(k_pad, start, band, axis=1)
        vc = lax.dynamic_slice_in_dim(v_pad, start, band, axis=1)
        s = jnp.einsum('bqhd,bkhd->bhqk', qc, kc).astype(jnp.float32) * scale + bias
        valid = jnp.arange(band) >= (pad - start)
        s = jnp.where(valid, s, -jnp.inf)
        p = jax.nn.softmax(s, axis=-1)
        return jnp.einsum('bhqk,bkhd->bqhd', p.astype(vc.dtype), vc)

    out = lax.map(one_chunk, (jnp.arange(nc), q_chunks))
    return jnp.moveaxis(out, 0, 1).reshape(B_, S, H * Dh)

def hybrid_mixer(x, positions, w_in, conv_w, rel_bias, w_out):
    B_, S, _ = x.shape
    proj = jnp.einsum('bsd,dp->bsp', x, w_in)
    offs = np.cumsum(np.array(IN_SIZES_2))[:-1].tolist()
    (cb, cc, ch, dq, dk, dv, iq, ik, iw, cq, ck, cv) = jnp.split(proj, offs, axis=-1)
    y_conv = short_conv_mixer(cb, cc, ch, conv_w)
    dq = partial_rope(dq.reshape(B_, S, DSA_HEADS, HEAD_DIM), positions, ROPE_DIM)
    dk = partial_rope(dk.reshape(B_, S, 1, HEAD_DIM), positions, ROPE_DIM)[:, :, 0]
    iq = partial_rope(iq.reshape(B_, S, IDX_HEADS, IDX_DIM), positions, IDX_ROPE_DIM)
    ik = partial_rope(ik.reshape(B_, S, 1, IDX_DIM), positions, IDX_ROPE_DIM)[:, :, 0]
    y_dsa = dsa_attention(dq, dk, dv, iq, ik, iw)
    cq = cq.reshape(B_, S, CHK_HEADS, HEAD_DIM)
    ck = ck.reshape(B_, S, CHK_HEADS, HEAD_DIM)
    cv = cv.reshape(B_, S, CHK_HEADS, HEAD_DIM)
    y_chk = chunk_band_attention(cq, ck, cv, rel_bias)
    y = jnp.concatenate([y_conv, y_dsa, y_chk], axis=-1)
    return jnp.einsum('bsm,md->bsd', y, w_out)

def memory_cross_attention(x, mem, w_q, w_kv, w_o):
    B_, S, _ = x.shape
    M = mem.shape[1]
    q = jnp.einsum('bsd,de->bse', x, w_q).reshape(B_, S, MEM_HEADS, MEM_HEAD_DIM)
    k, v = jnp.split(jnp.einsum('bmd,de->bme', mem, w_kv), 2, axis=-1)
    k = k.reshape(B_, M, MEM_HEADS, MEM_HEAD_DIM)
    v = v.reshape(B_, M, MEM_HEADS, MEM_HEAD_DIM)
    s = jnp.einsum('bshd,bmhd->bhsm', q, k).astype(jnp.float32) * (MEM_HEAD_DIM ** -0.5)
    p = jax.nn.softmax(s, axis=-1)
    o = jnp.einsum('bhsm,bmhd->bshd', p.astype(v.dtype), v).reshape(B_, S, D_MODEL)
    return jnp.einsum('bse,ed->bsd', o, w_o)

def squared_relu_mlp(x, w1, w2):
    h = jnp.square(jax.nn.relu(jnp.einsum('bsd,df->bsf', x, w1)))
    return jnp.einsum('bsf,fd->bsd', h, w2)

def second_inputs(seed: int = 0) -> dict:
    key = jax.random.key(seed)
    ks = jax.random.split(key, 20)
    f32 = jnp.float32
    nrm = lambda k, shape, s: jax.random.normal(k, shape, f32) * s
    x = nrm(ks[0], (BATCH, SEQ, D_MODEL), 1.0)
    mem = nrm(ks[1], (BATCH, MEM_LEN, D_MODEL), 1.0)
    offset = jax.random.randint(ks[2], (BATCH,), 0, 4096, dtype=jnp.int32)
    positions = (offset[:, None] + jnp.arange(SEQ, dtype=jnp.int32)[None, :]).astype(jnp.int32)
    return {
        'x': x,
        'mem': mem,
        'positions': positions,
        'w_in': nrm(ks[3], (DEPTH, D_MODEL, IN_WIDTH), D_MODEL ** -0.5),
        'conv_w': nrm(ks[4], (DEPTH, CONV_K, CONV_WIDTH), CONV_K ** -0.5),
        'rel_bias': nrm(ks[5], (DEPTH, CHK_HEADS, REL_SIZE), 0.5),
        'w_mix_out': nrm(ks[6], (DEPTH, MIX_WIDTH, D_MODEL), BETA * MIX_WIDTH ** -0.5),
        'ln1_g': 1.0 + nrm(ks[7], (DEPTH, D_MODEL), 0.02),
        'ln1_b': nrm(ks[8], (DEPTH, D_MODEL), 0.02),
        'w_mq': nrm(ks[9], (DEPTH, D_MODEL, D_MODEL), D_MODEL ** -0.5),
        'w_mkv': nrm(ks[10], (DEPTH, D_MODEL, 2 * D_MODEL), D_MODEL ** -0.5),
        'w_mo': nrm(ks[11], (DEPTH, D_MODEL, D_MODEL), BETA * D_MODEL ** -0.5),
        'ln2_g': 1.0 + nrm(ks[12], (DEPTH, D_MODEL), 0.02),
        'ln2_b': nrm(ks[13], (DEPTH, D_MODEL), 0.02),
        'w_ff1': nrm(ks[14], (DEPTH, D_MODEL, D_FF), D_MODEL ** -0.5),
        'w_ff2': nrm(ks[15], (DEPTH, D_FF, D_MODEL), BETA * D_FF ** -0.5),
        'ln3_g': 1.0 + nrm(ks[16], (DEPTH, D_MODEL), 0.02),
        'ln3_b': nrm(ks[17], (DEPTH, D_MODEL), 0.02),
    }

def second_block(x, mem, positions, w_in, conv_w, rel_bias, w_mix_out, ln1_g, ln1_b,
              w_mq, w_mkv, w_mo, ln2_g, ln2_b, w_ff1, w_ff2, ln3_g, ln3_b):
    for l in range(DEPTH):
        mix = hybrid_mixer(x, positions, w_in[l], conv_w[l], rel_bias[l], w_mix_out[l])
        x = layer_norm(ALPHA * x + mix, ln1_g[l], ln1_b[l])
        cross = memory_cross_attention(x, mem, w_mq[l], w_mkv[l], w_mo[l])
        x = layer_norm(ALPHA * x + cross, ln2_g[l], ln2_b[l])
        ff = squared_relu_mlp(x, w_ff1[l], w_ff2[l])
        x = layer_norm(ALPHA * x + ff, ln3_g[l], ln3_b[l])
    return x


def setup_inputs(seed=0):
    out = dict(first_inputs(seed))
    for name, value in second_inputs(seed + 1).items():
        if name != "x":
            out[name + "_2"] = value
    return out


def reference(
    x, c, ctx, c_ctx, w_ada, b_ada, g_norm1, w_in, gq_a, gk_a, gq_b, gk_b, rpb_b, gq_c, gk_c,
    lambda_q1, lambda_k1, lambda_q2, lambda_k2, g_subln, w_out, g_norm2, w_up, conv_w, conv_b,
    w_down, mem_2, positions_2, w_in_2, conv_w_2, rel_bias_2, w_mix_out_2, ln1_g_2, ln1_b_2,
    w_mq_2, w_mkv_2, w_mo_2, ln2_g_2, ln2_b_2, w_ff1_2, w_ff2_2, ln3_g_2, ln3_b_2,
):
    x = first_block(
        x, c, ctx, c_ctx, w_ada, b_ada, g_norm1, w_in, gq_a, gk_a, gq_b, gk_b, rpb_b, gq_c,
        gk_c, lambda_q1, lambda_k1, lambda_q2, lambda_k2, g_subln, w_out, g_norm2, w_up, conv_w,
        conv_b, w_down,
    )
    return second_block(
        x, mem_2, positions_2, w_in_2, conv_w_2, rel_bias_2, w_mix_out_2, ln1_g_2, ln1_b_2,
        w_mq_2, w_mkv_2, w_mo_2, ln2_g_2, ln2_b_2, w_ff1_2, w_ff2_2, ln3_g_2, ln3_b_2,
    )


_drawn_inputs = setup_inputs


def setup_inputs(seed=0):
    import zlib

    import numpy as np

    out = dict(_drawn_inputs(seed))
    spreads = {}
    factors = {'b_ada': 3.048,
     'g_norm1': 8.0,
     'gq_a': 8.0,
     'gk_a': 8.0,
     'gq_b': 8.0,
     'gk_b': 8.0,
     'rpb_b': 8.0,
     'gq_c': 8.0,
     'gk_c': 8.0,
     'lambda_q1': 8.0,
     'lambda_k1': 8.0,
     'lambda_q2': 8.0,
     'lambda_k2': 6.825,
     'g_subln': 21.672,
     'g_norm2': 8.0,
     'conv_b': 8.0,
     'rel_bias_2': 3.241}
    for name, (base, spread) in spreads.items():
        noise = np.random.default_rng([zlib.crc32(name.encode()), seed]).standard_normal(out[name].shape)
        drawn = base * np.exp(spread * noise) if base else spread * noise
        out[name] = __import__('jax').numpy.asarray(drawn.astype(out[name].dtype))
    for name, factor in factors.items():
        out[name] = (out[name] * factor).astype(out[name].dtype)
    return out
```

```python
import math
from contextlib import ExitStack

import numpy as np
import concourse.bass as bass
from concourse import mybir

F32 = mybir.dt.float32
F32R = mybir.dt.float32r
I32 = mybir.dt.int32
ALU = mybir.AluOpType
ACT = mybir.ActivationFunctionType
AX = mybir.AxisListType

P = 128
D = 1024
KT = D // P
SEQ = 512
CTX = 256
MEM = 256
DEPTH = 2
GRID_W = 64
HEAD = 64
WIN_W = 16
B_HEADS = 4
FFN = 2816
FT = FFN // P
EPS = 1e-6
LN_EPS = 1e-5
ALPHA = (2.0 * DEPTH) ** 0.25
D_FF = 4096
NEG = -1e30
TAKEN = -3e38
REL_CLIP, CHUNK = 128, 64
REL_SIZE = (CHUNK - 1) + REL_CLIP + 1
TOPK = 128
NRAW = 3
NSPLIT = 3
AHEAD = 2


def axial_tables(dim):
    half = dim // 2
    inv = (10000.0 ** (-np.arange(0, half, 2, dtype=np.float32) / half)).astype(np.float32)
    t = np.arange(SEQ)
    row, col = (t // GRID_W).astype(np.float32), (t % GRID_W).astype(np.float32)
    ang = np.concatenate([row[:, None] * inv, col[:, None] * inv], axis=-1).astype(np.float32)
    full = np.tile(np.repeat(ang, 2, axis=1), (1, P // dim)).T
    return np.cos(full).astype(np.float32), np.sin(full).astype(np.float32)


def constant_arrays():
    i = np.arange(P)
    eye = (i[:, None] == i[None, :]).astype(np.float32)
    mean = np.full((P, P), 1.0 / D, np.float32)
    blk64 = (i[:, None] // 64 == i[None, :] // 64).astype(np.float32)
    blk32 = (i[:, None] // 32 == i[None, :] // 32).astype(np.float32)
    pair = np.zeros((P, P), np.float32)
    pair[i[::2] + 1, i[::2]] = -1.0
    pair[i[::2], i[::2] + 1] = 1.0
    half_d = np.zeros((P, P), np.float32)
    freq = np.zeros((P, 2), np.float32)
    half_i = np.zeros((P, P), np.float32)
    for mat, period, half, c in ((half_d, 64, 8, 0), (half_i, 32, 4, 1)):
        inv = np.power(np.float32(500000.0), -np.arange(half, dtype=np.float32) / half).astype(np.float32)
        for b in range(0, P, period):
            for j in range(half):
                mat[b + j + half, b + j] = -1.0
                mat[b + j, b + j + half] = 1.0
                freq[b + j, c] = freq[b + j + half, c] = inv[j]
    q = np.arange(P) % 64
    start = np.clip(q - WIN_W // 2, 0, GRID_W - WIN_W)
    kc = np.arange(GRID_W)
    inside = (kc[None, :] >= start[:, None]) & (kc[None, :] < start[:, None] + WIN_W)
    window = np.where(inside, 0.0, NEG).astype(np.float32)
    causal = np.where(i[None, :] // CHUNK <= i[:, None] // CHUNK, 0.0, NEG).astype(np.float32)
    pack = np.concatenate([eye, mean, blk64, blk32, pair, half_d, half_i, causal, window, freq], axis=1)
    ca, sa = axial_tables(64)
    cc, sc = axial_tables(32)
    return {"const_pack": pack, "const_rope": np.stack([ca, sa, cc, sc], axis=1)}


def param_columns():
    cols, n = {}, 0
    for name, rows in (("b_ada", 2 * 48), ("g_norm1", 16), ("g_norm2", 16), ("conv_w", 2 * 3 * 2 * FT),
                       ("conv_b", 2 * 2 * FT), ("conv_w_2", 2 * 3 * 2), ("ln1_g_2", 16), ("ln1_b_2", 16),
                       ("ln2_g_2", 16), ("ln2_b_2", 16), ("ln3_g_2", 16), ("ln3_b_2", 16), ("c", 8),
                       ("c_ctx", 8), ("gains", 12)):
        cols[name] = (n, rows)
        n += rows
    return cols, n


PCOL, NPARAM = param_columns()
NGRP = -(-NPARAM // P)
GAINS = ("gq_a", "gk_a", "gq_b", "gk_b", "gq_c", "gk_c")


def weight_chunks():
    chunks, first = [], {}

    def add(key, name, layer, k0, nk, pieces):
        first.setdefault(key, len(chunks))
        chunks.append((name, layer, k0, nk, pieces))

    def cols(c):
        return [(0, P, c)]

    for l in range(DEPTH):
        for n in range(48):
            add(("ada", l), "w_ada", l, 0, KT, cols(n * P))
    for l in range(DEPTH):
        for s in ("c", "x"):
            for tile in qkv_tiles(s, l):
                add(("qkv", s, l), "w_in", l, 0, KT, tile["pieces"])
        for s in streams(l):
            for n in range(KT):
                add(("out", s, l), "w_out", l, 0, KT, cols(n * P))
        for s in streams(l):
            for step in ffn_steps(GROUPS_1, 2):
                if step[0] == "up":
                    _, g, j, part = step
                    add(("ffn", s, l), "w_up", l, 0, KT, cols(part * FFN + (GROUPS_1[g][0] + j) * P))
                else:
                    _, g, n = step
                    add(("ffn", s, l), "w_down", l, GROUPS_1[g][0], GROUPS_1[g][1], cols(n * P))
    for l in range(DEPTH):
        for tile in mixer_tiles():
            add(("mix_in", l), "w_in_2", l, 0, KT, tile["pieces"])
        for n in range(KT):
            add(("mix_out", l), "w_mix_out_2", l, 0, KT, cols(n * P))
        for n in range(2 * KT):
            add(("mem_kv", l), "w_mkv_2", l, 0, KT, cols(n * P))
        for n in range(KT):
            add(("mem_q", l), "w_mq_2", l, 0, KT, cols(n * P))
        for n in range(KT):
            add(("mem_out", l), "w_mo_2", l, 0, KT, cols(n * P))
        for step in ffn_steps(GROUPS_2, 1):
            if step[0] == "up":
                _, g, j, _ = step
                add(("ff", l), "w_ff1_2", l, 0, KT, cols((GROUPS_2[g][0] + j) * P))
            else:
                _, g, n = step
                add(("ff", l), "w_ff2_2", l, GROUPS_2[g][0], GROUPS_2[g][1], cols(n * P))
    return chunks, first


def streams(layer):
    return ("x", "c")[:DEPTH - layer]


TOKENS = {"x": SEQ, "c": CTX}
GROUPS_1 = [(0, 8), (8, 8), (16, 6)]
GROUPS_2 = [(0, 8), (8, 8), (16, 8), (24, 8)]


def ffn_steps(groups, parts):
    steps = []
    for g in range(len(groups) + 1):
        if g < len(groups):
            steps += [("up", g, j, part) for j in range(groups[g][1]) for part in range(parts)]
        if g:
            steps += [("down", g - 1, n) for n in range(KT)]
    return steps


def qkv_tiles(stream, layer):
    only_kv = stream == "c" and layer == DEPTH - 1
    tiles = []

    def qk(slot, gain, blk, rope, pieces):
        if gain % 2 or not only_kv:
            tiles.append(dict(kind="qk", slot=slot, gain=gain, blk=blk, rope=rope, pieces=pieces))

    for m in range(4):
        qk(m, 0, 0, 0, [(0, 64, 64 * m), (64, 64, 256 + 64 * m)])
    qk(4, 1, 0, 0, [(0, P, 512)])
    for m in range(2):
        qk(5 + m, 2, 0, None, [(0, P, 768 + P * m)])
        qk(7 + m, 3, 0, None, [(0, P, 1024 + P * m)])
    for m in range(2):
        qk(9 + m, 4, 1, 2, [(0, P, 1536 + P * m)])
        qk(11 + m, 5, 1, 2, [(0, P, 1792 + P * m)])
    for n, c in enumerate((640, 1280, 1408, 2048, 2176)):
        tiles.append(dict(kind="v", col=n * P, pieces=[(0, P, c)]))
    if stream == "c":
        for t in tiles:
            t["rope"] = None
    return tiles


def is_value(tile):
    return tile["kind"] in ("v", "dv")


def aux_before(tiles, j):
    before = [m for m in range(j) if m % 2 == j % 2 and ("blk" in tiles[m] or is_value(tiles[m]))]
    return before[-1] if before else None


def mixer_tiles():
    t = [dict(kind="qk", slot=m, rope=0, scale=0.125, pieces=[(0, P, 768 + P * m)]) for m in range(3)]
    t.append(dict(kind="qk", slot=3, rope=0, scale=1.0, pieces=[(0, 64, 1152), (64, 64, 1152)]))
    t += [dict(kind="qk", slot=4 + m, rope=2, scale=1.0, pieces=[(0, P, 1280 + P * m)]) for m in range(2)]
    t.append(dict(kind="qk", slot=6, rope=2, scale=1.0, pieces=[(32 * j, 32, 1536) for j in range(4)]))
    t.append(dict(kind="dv", pieces=[(0, 64, 1216), (64, 64, 1568)]))
    t += [dict(kind="plain", slot=7 + m, scale=0.125, pieces=[(0, P, 1576 + P * m)]) for m in range(3)]
    t += [dict(kind="plain", slot=10 + m, scale=1.0, pieces=[(0, P, 1960 + P * m)]) for m in range(3)]
    t += [dict(kind="v", col=m * P, pieces=[(0, P, 2344 + P * m)]) for m in range(3)]
    t += [dict(kind="plain", slot=13 + m, scale=1.0, pieces=[(0, P, P * m)]) for m in range(6)]
    return t


CHUNKS, FIRST = weight_chunks()


def is_split(c):
    return CHUNKS[c][0] != "w_ada"


INDEX_STEPS = [(t, h) for t in range(1, 4) for h in range(8)]
ROUND = 12582912.0
TWO_PI_PARTS = (6.28125, float(np.float32(0.00193500518798828125)), 2 * math.pi - 6.28125 - 0.00193500518798828125)
SIN_MAX = 3.1415925


def build(nc, A, out, counts):
    ctx = ExitStack()
    totals = {}
    sems = {}

    def sem(name):
        sems[name] = ctx.enter_context(nc.semaphore(name))
        return name

    def mark(name, key, by=1):
        totals[name] = totals.get(name, 0) + by
        assert (name, key) not in marked, (name, key)
        marked.add((name, key))
        counts[name, key] = totals[name]
        return sems[name], by

    def at(name, key):
        if strict:
            return sems[name], counts[name, key]
        return sems[name], counts.get((name, key), 1)

    marked = set()
    strict = bool(counts)

    with ctx:
        def sb(name, shape, dt=F32, where=ctx):
            return where.enter_context(nc.sbuf_tensor(name, shape, dt))

        XT = sb("x_t", [P, KT, SEQ])
        CT = sb("ctx_t", [P, KT, CTX])
        HH = sb("h_hi", [P, KT, SEQ], F32R)
        HL = sb("h_lo", [P, KT, SEQ], F32R)
        RAW = sb("w_raw", [P, NRAW, KT, P])
        WH = sb("w_hi", [P, NSPLIT, KT, P], F32R)
        WL = sb("w_lo", [P, NSPLIT, KT, P], F32R)
        ACC = sb("acc", [P, SEQ])
        RSTD = sb("rstd", [P, SEQ])
        WORK = sb("work", [P, 2304])
        PACK = sb("const_sb", [P, 8 * P + 64 + 2])
        PRM = sb("params", [P, NGRP, P])
        MOD = sb("mod", [P, DEPTH, 48, 2])
        GMOD = sb("gain_mod", [P, DEPTH, 2, 2, KT])
        SILU = sb("silu_c", [P, KT, 2])
        HG = sb("head_gain", [P, 2, 6])
        LAMV = sb("lam_vec", [P, 2, 4, 32])
        LAM = sb("lam", [P, 2, 4])
        GSUB = sb("g_sub", [P, 2, HEAD])
        RELC = sb("rel_const", [P, 12])
        EPSC = sb("eps_cols", [P, 4])
        NMAX = sb("neg_max", [P, 4])
        SUMS = sb("prob_sums", [P, 2, 16])
        RSUM = sb("recip_sums", [P, 2, 16])
        COEF = sb("diff_coef", [P, 4])
        SSQ = sb("sub_sumsq", [P, 2, 4])
        TOP8 = sb("top8", [P, 8])
        IW = sb("idx_weights", [P, 4, 8])
        PS = ctx.enter_context(nc.psum_tensor("psum", [P, 8, 512], F32))

        IDENT, MEAN, BLK64, BLK32, PAIR, HALF_D, HALF_I, CAUSAL = (PACK[:, i * P:(i + 1) * P] for i in range(8))
        WINDOW = PACK[:, 8 * P:8 * P + 64]
        FREQ = PACK[:, 8 * P + 64:8 * P + 66]
        BLK = (BLK64, BLK32)
        SQ = [WORK[:, 512 * i:512 * i + 512] for i in range(2)]
        TMP = [WORK[:, 1024 + 512 * i:1536 + 512 * i] for i in range(2)]
        PROB = [WORK[:, 768 * i:768 * i + 768] for i in range(3)]

        def prm(name, i):
            c = PCOL[name][0] + i
            return PRM[:, c // P, c % P:c % P + 1]

        def prm_range(name, i, n):
            c = PCOL[name][0] + i
            return PRM[:, :, :].rearrange("p g c -> p (g c)")[:, c:c + n]

        ph = ExitStack()
        XN = sb("x_nat", [P, 6, D], where=ph)
        PROWS = sb("param_rows", [P, NGRP, P], where=ph)
        RPBR = sb("rpb_rows", [120, P], where=ph)
        RELR = sb("rel_rows", [12, 384], where=ph)
        ph.close()
        ph = ExitStack()
        MROW = sb("mod_rows_sb", [2, 2 * 6 * D], where=ph)
        ph.close()
        ph = ExitStack()
        QK = sb("qk_t", [P, 13, SEQ + CTX], where=ph)
        VN = sb("v_nat", [P, 6, 640], where=ph)
        TB = sb("win_bias", [P, B_HEADS, 14, GRID_W], where=ph)
        ROPE = sb("rope_1", [P, 4, SEQ], where=ph)
        PT = sb("probs_t", [P, 2, 6 * P], where=ph)
        ON = sb("o_nat", [P, 2, D], where=ph)
        ph.close()
        ph = ExitStack()
        GH = sb("hid_hi", [P, 2, 8, SEQ], F32R, where=ph)
        GL = sb("hid_lo", [P, 2, 8, SEQ], F32R, where=ph)
        MU = sb("mid_u", [P, 3, SEQ], where=ph)
        MG = sb("mid_g", [P, 3, SEQ], where=ph)
        ph.close()
        ph = ExitStack()
        QK2 = sb("qk_t_2", [P, 19, SEQ], where=ph)
        VN2 = sb("v_nat_2", [P, 4, 384], where=ph)
        DV = sb("dv_nat", [P, 4, P], where=ph)
        ROPE2 = sb("rope_2", [P, 4, SEQ], where=ph)
        TBK = sb("rel_bias_t", [P, 6, 256], where=ph)
        DMASK = sb("sel_mask", [P, 4, SEQ], where=ph)
        SCORE = sb("idx_score", [P, SEQ], where=ph)
        PT2 = sb("probs_t_2", [P, 2, 4 * P], where=ph)
        ON2 = sb("o_nat_2", [P, 2, 768], where=ph)
        POSI = sb("pos_int", [P, SEQ], I32, where=ph)
        ph.close()
        ph = ExitStack()
        MQ = sb("mem_q_t", [P, KT, SEQ], where=ph)
        MK = sb("mem_k_t", [P, KT, MEM], where=ph)
        MV = sb("mem_v", [P, 2, D], where=ph)
        MH = sb("mem_hi", [P, KT, MEM], F32R, where=ph)
        ML = sb("mem_lo", [P, KT, MEM], F32R, where=ph)
        PT3 = sb("probs_t_3", [P, 2, 2 * P], where=ph)
        ON3 = sb("o_nat_3", [P, 2, D], where=ph)
        ph.close()
        ph = ExitStack()
        OUTS = sb("out_nat", [P, 4, D], where=ph)
        ph.close()

        RPB_PAD = nc.dram_tensor("rpb_pad", (120, 64, P), F32).ap()
        REL_PAD = nc.dram_tensor("rel_pad", (12, P, 384), F32).ap()

        for i in range(NRAW):
            sem(f"w_loaded{i}")
        for name in ("w_hi", "w_lo", "w_used", "stage_end", "consts_in", "rows_in", "acts_in", "mem_in", "bias_in",
                     "tab_in", "bias2_in", "pad_written", "zeroed", "x_ready", "mod_rows", "v_turned", "mem_hi_made", "mem_lo_made", "turned", "turned_taken", "param_step", "param_act",
                     "ada_done", "sq_ready", "sum_step", "stat_done", "std_ready", "norm_step", "norm_mid", "h_hi", "h_lo",
                     "lin_done", "raw_copied", "raw_squared", "v_copied", "blk_done", "blk_std", "qk_step",
                     "rot_done", "rope_step", "scores_done", "bias_step", "neg_max", "exp_done", "mix_step", "probs_turned_a",
                     "probs_turned_b", "pt_copied_a", "pt_copied_b", "pv_done", "o_step", "sub_std", "o_turned_a",
                     "o_turned_b", "o_hi", "o_lo", "resid", "mid_ready", "conv_step", "silu_ready", "prod_ready", "hid_hi",
                     "hid_lo", "down_done", "trig_step", "trig_act", "idx_done", "idx_relu", "idx_step",
                     "cv_step", "cv_hi", "out_turned", "out_copied", "out_stored"):
            sem(name)

        block = ctx.enter_context(nc.Block())

        @block.sync
        def _(sp):
            for c, (name, layer, k0, nk, pieces) in enumerate(CHUNKS):
                if c >= NRAW:
                    sp.wait_ge(*at("w_lo" if is_split(c - NRAW) else "w_used", c - NRAW))
                for n, (dst, width, src) in enumerate(pieces):
                    w = A[name][layer, k0 * P:(k0 + nk) * P, src:src + width].rearrange("(k p) n -> p k n", p=P)
                    key = c if n == len(pieces) - 1 else (c, n)
                    sp.dma_start(RAW[:, c % NRAW, 0:nk, dst:dst + width], w).then_inc(
                        *mark(f"w_loaded{c % NRAW}", key, 16))

        @block.gpsimd
        def _(pool):
            for c, (_, _, _, nk, _) in enumerate(CHUNKS):
                if not is_split(c):
                    continue
                pool.wait_ge(*at("w_hi", c))
                nc.gpsimd.tensor_tensor(WL[:, c % NSPLIT, 0:nk, :], RAW[:, c % NRAW, 0:nk, :],
                                        WH[:, c % NSPLIT, 0:nk, :].bitcast(F32), ALU.subtract).then_inc(
                                            *mark("w_lo", c))

        def lin_bank(i):
            return i % 4

        def wide(values, col, head):
            fits = col + P <= values.shape[1] and (head + 2) * HEAD <= 512
            return values[:, col:col + (P if fits else HEAD)]

        def attention_units_1(stream, layer):
            units, groups = [], []
            tiles = range(4) if stream == "x" else range(2)
            nk = SEQ + CTX if stream == "x" else CTX
            k0 = 0 if stream == "x" else SEQ
            vt = range(6) if stream == "x" else range(4, 6)
            q0 = 0 if stream == "x" else SEQ
            for t in tiles:
                qc = slice(q0 + t * P, q0 + (t + 1) * P)

                def one(slot_q, slot_k, part, rows):
                    return [(QK[part:part + rows, slot_q, qc], QK[part:part + rows, slot_k, k0:k0 + nk])]

                for h in range(8):
                    part, slot = 64 * (h // 4), h % 4
                    units.append(dict(maps=[one(slot, 4, part, 64)], nk=nk, adds=[],
                                      v=[wide(VN[:, j, :], 64 * (h // 4), h) for j in vt],
                                      t=t, group=len(groups), head=h, dv=64, last=h == 7))
                groups.append(dict(heads=8, dv=64, col=0, diff=False))
                for h in range(4):
                    part = 64 * (h % 2)
                    adds = []
                    if stream == "x":
                        bias = TB[:, h, 6 - 2 * t:14 - 2 * t, :].rearrange("p a b -> p (a b)")
                        adds = [(0, SEQ, bias)]
                    units.append(dict(maps=[one(5 + h // 2, 7 + h // 2, part, 64)], nk=nk, adds=adds,
                                      v=[wide(VN[:, j, :], P + 64 * h, h) for j in vt],
                                      t=t, group=len(groups), head=h, dv=64, last=h == 3))
                groups.append(dict(heads=4, dv=64, col=512, diff=False))
                for h in range(4):
                    part = 64 * (h % 2)
                    units.append(dict(maps=[one(9 + h // 2, 11 + h // 2, part + 32 * m, 32) for m in range(2)],
                                      nk=nk, adds=[], v=[wide(VN[:, j, :], 384 + 64 * h, h) for j in vt],
                                      t=t, group=len(groups), head=h, dv=64, last=h == 3))
                groups.append(dict(heads=4, dv=64, col=768, diff=True, layer=layer))
                units[-1]["tile_last"] = True
            return dict(units=units, groups=groups, PT=PT, ON=ON, tiles=8, first=0)

        def attention_units_2(layer):
            units, groups = [], []
            for t in range(4):
                nk = P * (t + 1)
                qc = slice(t * P, (t + 1) * P)
                for h in range(6):
                    part = 64 * (h % 2)
                    units.append(dict(maps=[[(QK2[part:part + 64, 7 + h // 2, qc], QK2[part:part + 64, 10 + h // 2, 0:nk])]],
                                      nk=nk,
                                      adds=([(0, P, TBK[:, h, P:2 * P])] if t == 0 else
                                            ([(0, nk - 2 * P, RELC[:, layer * 6 + h:layer * 6 + h + 1])] if t > 1 else [])
                                            + [(nk - 2 * P, nk, TBK[:, h, :])]),
                                      v=[wide(VN2[:, j, :], 64 * h, h) for j in range(t + 1)],
                                      t=t, group=len(groups), head=h, dv=64, last=h == 5))
                groups.append(dict(heads=6, dv=64, col=384, diff=False))
                for h in range(6):
                    part = 64 * (h % 2)
                    units.append(dict(maps=[[(QK2[part:part + 64, h // 2, qc], QK2[part:part + 64, 3, 0:nk])]],
                                      nk=nk, adds=[(0, nk, DMASK[:, t, 0:nk])],
                                      v=[wide(DV[:, j, :], 0, h) for j in range(t + 1)],
                                      t=t, group=len(groups), head=h, dv=64, last=h == 5))
                groups.append(dict(heads=6, dv=64, col=0, diff=False))
                units[-1]["tile_last"] = True
            return dict(units=units, groups=groups, PT=PT2, ON=ON2, tiles=6, first=2)

        def attention_units_3():
            units, groups = [], []
            for t in range(4):
                qc = slice(t * P, (t + 1) * P)
                for h in range(4):
                    units.append(dict(maps=[[(MQ[:, 2 * h + i, qc], MK[:, 2 * h + i, :]) for i in range(2)]],
                                      nk=MEM, adds=[], v=[MV[:, j, 256 * h:256 * h + 256] for j in range(2)],
                                      t=t, group=len(groups), head=h % 2, dv=256, last=h % 2 == 1))
                    if h % 2:
                        groups.append(dict(heads=2, dv=256, col=256 * (h - 1), diff=False))
                units[-1]["tile_last"] = True
            return dict(units=units, groups=groups, PT=PT3, ON=ON3, tiles=8, first=0)

        def number_attention(S, att):
            n, uses = 0, {}
            units = att["units"]
            for u, unit in enumerate(units):
                unit["sub"] = list(range(n, n + len(unit["maps"])))
                n += len(unit["maps"])
            k = 0
            for i in range(len(units) + 5):
                if 0 <= i - 1 < len(units):
                    uses["unit", i - 1] = k
                    k += 1
                if 0 <= i - 4 < len(units) and units[i - 4].get("tile_last"):
                    uses["tile", units[i - 4]["t"]] = k
                    k += 1
            att["S"], att["uses"], att["order"] = S, uses, {v: k for k, v in uses.items()}
            return att

        @block.tensor
        def _(pe):
            stage = [0]

            def stage_end():
                stage[0] += 1
                pe.drain().then_inc(*mark("stage_end", ("pe", stage[0])))
                pe.wait_ge(sems["stage_end"], 3 * stage[0])

            def product(out_ap, lhs, rhs, nk):
                for k in range(nk):
                    for n, (a, b) in enumerate(((0, 0), (0, 1), (1, 0))):
                        m = pe.matmul(out_ap, lhs(a, k), rhs(b, k), start=(k == 0 and n == 0),
                                      stop=(k == nk - 1 and n == 2))
                return m

            def weights(c):
                w = (WH[:, c % NSPLIT], WL[:, c % NSPLIT])
                pe.wait_ge(*at("w_lo", c))
                return w

            def tile_t(c, out_ap, acts, T, nk=KT):
                w = weights(c)
                product(out_ap, lambda a, k: w[a][:, k, :], lambda b, k: acts[b][:, k, 0:T], nk).then_inc(
                    *mark("w_used", c))

            H = (HH, HL)

            def turn_in(S, n):
                for i in range(n):
                    for half in range(2):
                        b = (2 * i + half) % 8
                        if 2 * i + half >= 8:
                            pe.wait_ge(*at("turned_taken", (S, 2 * i + half - 8)))
                        for k in range(4):
                            m = pe.transpose(PS[:, b, k * P:(k + 1) * P], XN[:, i, (4 * half + k) * P:(4 * half + k + 1) * P],
                                             IDENT)
                        m.then_inc(*mark("turned", (S, 2 * i + half)))

            def stat(S, T, bank=0):
                pe.wait_ge(*at("sum_step", (S, "total")))
                pe.matmul(PS[:, bank, 0:T], MEAN, ACC[:, 0:T], start=True, stop=True).then_inc(
                    *mark("stat_done", S))

            def aux_bank_free(S, tiles, j):
                p = aux_before(tiles, j)
                if p is not None:
                    pe.wait_ge(*at("v_copied" if is_value(tiles[p]) else "blk_std", (S, p)))

            def turn_values(S, j, T):
                for t in range(T // P):
                    m = pe.transpose(PS[:, 4 + j % 2, t * P:(t + 1) * P], SQ[j % 2][:, t * P:(t + 1) * P], IDENT)
                m.then_inc(*mark("v_turned", (S, j)))

            def project(S, tiles, c0, T, rots):
                n = len(tiles)
                for i in range(n + 2):
                    if i < n:
                        if i >= 4:
                            pe.wait_ge(*at("raw_copied", (S, i - 4)))
                        tile_t(c0 + i, PS[:, lin_bank(i), 0:T], H, T)
                    j = i - 1
                    if 0 <= j < n and tiles[j]["kind"] == "qk" and "blk" in tiles[j]:
                        pe.wait_ge(*at("raw_squared", (S, j)))
                        aux_bank_free(S, tiles, j)
                        pe.matmul(PS[:, 4 + j % 2, 0:T], BLK[tiles[j]["blk"]], SQ[j % 2][:, 0:T], start=True,
                                  stop=True).then_inc(*mark("blk_done", (S, j)))
                    if 0 <= j < n and is_value(tiles[j]):
                        pe.wait_ge(*at("raw_copied", (S, j)))
                        aux_bank_free(S, tiles, j)
                        turn_values(S, j, T)
                    j = i - 2
                    if 0 <= j < n and tiles[j]["kind"] == "qk" and tiles[j]["rope"] is not None:
                        if "blk" in tiles[j]:
                            pe.wait_ge(*at("qk_step", (S, j, "norm")))
                        else:
                            pe.wait_ge(*at("raw_copied", (S, j)))
                        prev = [m for m in range(j) if tiles[m]["kind"] == "qk" and tiles[m]["rope"] is not None
                                and m % 2 == j % 2]
                        if prev:
                            pe.wait_ge(*at("rope_step", (S, prev[-1], "sin")))
                        dst, off = (QK, SEQ if S[1] == "c" else 0) if len(S) > 2 else (QK2, 0)
                        pe.matmul(PS[:, 6 + j % 2, 0:T], rots[tiles[j]["rope"]], dst[:, tiles[j]["slot"], off:off + T],
                                  start=True, stop=True).then_inc(*mark("rot_done", (S, j)))

            def out_proj(S, c0, T):
                for n in range(KT):
                    if n >= 4:
                        pe.wait_ge(*at("resid", (S, n - 4)))
                    tile_t(c0 + n, PS[:, lin_bank(n), 0:T], H, T)

            def attend(att):
                S, units, groups, PTt, ONt = att["S"], att["units"], att["groups"], att["PT"], att["ON"]
                uses, order = att["uses"], att["order"]

                def bank_free(use, part, sem_u, sem_t):
                    prev = use - 1
                    while prev >= 0:
                        kind, idx = order[prev]
                        if kind == "tile" or part == "a" or units[idx]["nk"] > 512:
                            pe.wait_ge(*(at(sem_t, (S, idx, part)) if kind == "tile" else at(sem_u, (S, idx))))
                            return
                        prev -= 1

                for i in range(len(units) + 4):
                    if i < len(units):
                        u = units[i]
                        for s, pieces in zip(u["sub"], u["maps"]):
                            if s >= 2:
                                pe.wait_ge(*at("exp_done", (S, s - 2)))
                            for lo in range(0, u["nk"], 512):
                                hi = min(lo + 512, u["nk"])
                                for n, (q, k) in enumerate(pieces):
                                    m = pe.matmul(PS[:, 2 * (s % 2) + lo // 512, 0:hi - lo], q, k[:, lo:hi],
                                                  start=n == 0, stop=n == len(pieces) - 1)
                            m.then_inc(*mark("scores_done", (S, s)))
                    j = i - 1
                    if 0 <= j < len(units):
                        u = units[j]
                        if len(u["sub"]) == 2:
                            pe.wait_ge(*at("mix_step", (S, j, "mixed")))
                        else:
                            pe.wait_ge(*at("exp_done", (S, u["sub"][0])))
                        use = uses["unit", j]
                        bank_free(use, "a", "pt_copied_a", "o_lo")
                        src = PROB[u["sub"][0] % 3]
                        for kt in range(u["nk"] // P):
                            if kt == 4:
                                bank_free(use, "b", "pt_copied_b", "o_lo")
                            m = pe.transpose(PS[:, 4 + kt // 4, (kt % 4) * P:(kt % 4 + 1) * P],
                                             src[:, kt * P:(kt + 1) * P], IDENT)
                            if kt == min(4, u["nk"] // P) - 1:
                                m.then_inc(*mark("probs_turned_a", (S, j)))
                        if u["nk"] > 512:
                            m.then_inc(*mark("probs_turned_b", (S, j)))
                    j = i - 2
                    if 0 <= j < len(units):
                        u = units[j]
                        pe.wait_ge(*at("pt_copied_a", (S, j)))
                        if u["nk"] > 512:
                            pe.wait_ge(*at("pt_copied_b", (S, j)))
                        g = u["group"]
                        if u["head"] == 0 and g >= 2:
                            pe.wait_ge(*at("o_step", (S, g - 2, "scaled")))
                        col = u["head"] * u["dv"]
                        for kt, v in enumerate(u["v"]):
                            m = pe.matmul(PS[:, 6 + g % 2, col:col + v.shape[1]],
                                          PTt[:, j % 2, kt * P:(kt + 1) * P], v, start=kt == 0,
                                          stop=kt == len(u["v"]) - 1)
                        m.then_inc(*mark("pv_done", (S, j)))
                    j = i - 4
                    if 0 <= j < len(units) and units[j].get("tile_last"):
                        t = units[j]["t"]
                        g = units[j]["group"]
                        pe.wait_ge(*at("o_step", (S, g, "ready" if groups[g]["diff"] else "scaled")))
                        bank_free(uses["tile", t], "a", "pt_copied_a", "o_lo")
                        for k in range(att["tiles"]):
                            if k == 4:
                                bank_free(uses["tile", t], "b", "pt_copied_b", "o_lo")
                            m = pe.transpose(PS[:, 4 + k // 4, (k % 4) * P:(k % 4 + 1) * P],
                                             ONt[:, t % 2, k * P:(k + 1) * P], IDENT)
                            if k == 3:
                                m.then_inc(*mark("o_turned_a", (S, t)))
                        m.then_inc(*mark("o_turned_b", (S, t)))

            def ffn(S, c0, T, groups, parts):
                up = 0
                down = 0
                for n, step in enumerate(ffn_steps(groups, parts)):
                    if step[0] == "up":
                        if up >= 4:
                            if parts == 2:
                                pe.wait_ge(*at("conv_step", (S, up - 4, "after")))
                            else:
                                pe.wait_ge(*at("mid_ready", (S, up - 4)))
                        tile_t(c0 + n, PS[:, lin_bank(up), 0:T], H, T)
                        up += 1
                    else:
                        _, g, m = step
                        if down >= 4:
                            pe.wait_ge(*at("resid", (S, down - 4)))
                        if m == 0:
                            pe.wait_ge(*at("hid_lo", (S, groups[g][0] + groups[g][1] - 1)))
                        tile_t(c0 + n, PS[:, 4 + down % 4, 0:T], (GH[:, g % 2], GL[:, g % 2]), T, groups[g][1])
                        down += 1

            def layer_norm(S):
                stat((S, "mean"), SEQ, 0)
                stat((S, "var"), SEQ, 1)
                stage_end()

            pe.wait_ge(*at("consts_in", "last"))
            pe.wait_ge(*at("rows_in", "last"))
            for g in range(NGRP):
                m = pe.transpose(PS[:, 6 + g // 4, (g % 4) * P:(g % 4 + 1) * P], PROWS[:, g, :], IDENT)
            m.then_inc(*mark("turned", "params"))
            pe.wait_ge(*at("acts_in", "last"))
            pe.wait_ge(*at("turned_taken", "params"))
            turn_in("in", 6)
            pe.wait_ge(*at("param_act", "silu"))
            stage_end()
            for n in range(2 * 48):
                c = FIRST["ada", 0] + n
                if n % 4 == 0 and n >= 32:
                    pe.wait_ge(*at("mod_rows", n // 4 - 8))
                pe.wait_ge(*at(f"w_loaded{c % NRAW}", c))
                for k in range(KT):
                    m = pe.matmul(PS[0:2, n // 4 % 8, n % 4 * P:(n % 4 + 1) * P], SILU[:, k, :], RAW[:, c % NRAW, k, :],
                                  start=k == 0, stop=k == KT - 1)
                m.then_inc(*mark("w_used", c))
            pe.wait_ge(*at("mod_rows", 23))
            for n in range(2 * 48):
                m = pe.transpose(PS[:, n // 48, 2 * (n % 48):2 * (n % 48) + 2], MROW[:, n * P:(n + 1) * P],
                                 IDENT[0:2, 0:2])
            m.then_inc(*mark("turned", "mod"))
            stage_end()
            for l in range(DEPTH):
                for s in ("c", "x"):
                    stat(("n1", s, l), TOKENS[s])
                    stage_end()
                    project(("qkv", s, l), qkv_tiles(s, l), FIRST["qkv", s, l], TOKENS[s], {0: PAIR, 2: PAIR})
                    stage_end()
                for s in streams(l):
                    attend(number_attention(("att", s, l), attention_units_1(s, l)))
                    stage_end()
                    out_proj(("out", s, l), FIRST["out", s, l], TOKENS[s])
                    stage_end()
                for s in streams(l):
                    stat(("n2", s, l), TOKENS[s])
                    stage_end()
                    ffn(("ffn", s, l), FIRST["ffn", s, l], TOKENS[s], GROUPS_1, 2)
                    stage_end()
            pe.wait_ge(*at("mem_in", "last"))
            turn_in("mem", 2)
            stage_end()
            for l in range(DEPTH):
                project(("mix_in", l), mixer_tiles(), FIRST["mix_in", l], SEQ, {0: HALF_D, 2: HALF_I})
                stage_end()
                for n, (t, h) in enumerate(INDEX_STEPS):
                    if n >= 2:
                        pe.wait_ge(*at("idx_relu", (l, n - 2)))
                    pp = 32 * (h % 4)
                    pe.matmul(PS[:, n % 2, 0:(t + 1) * P], QK2[pp:pp + 32, 4 + h // 4, t * P:(t + 1) * P],
                              QK2[pp:pp + 32, 6, 0:(t + 1) * P], start=True, stop=True).then_inc(
                                  *mark("idx_done", (l, n)))
                stage_end()
                attend(number_attention(("att2", l), attention_units_2(l)))
                stage_end()
                out_proj(("mix_out", l), FIRST["mix_out", l], SEQ)
                stage_end()
                layer_norm(("ln1", l))
                kv = ("mem_kv", l)
                for n in range(2 * KT + 1):
                    if n >= 4:
                        pe.wait_ge(*at("raw_copied", (kv, n - 4)))
                    if n < 2 * KT:
                        tile_t(FIRST[kv] + n, PS[:, lin_bank(n), 0:MEM], (MH, ML), MEM)
                    if n > KT:
                        pe.wait_ge(*at("raw_copied", (kv, n - 1)))
                        if n > KT + 2:
                            pe.wait_ge(*at("v_copied", (kv, n - 3)))
                        turn_values(kv, n - 1, MEM)
                for n in range(KT):
                    pe.wait_ge(*(at("raw_copied", (kv, 2 * KT - 4 + n)) if n < 4 else
                                 at("raw_copied", (("mem_q", l), n - 4))))
                    tile_t(FIRST["mem_q", l] + n, PS[:, lin_bank(n), 0:SEQ], H, SEQ)
                stage_end()
                attend(number_attention(("att3", l), attention_units_3()))
                stage_end()
                out_proj(("mem_out", l), FIRST["mem_out", l], SEQ)
                stage_end()
                layer_norm(("ln2", l))
                ffn(("ff", l), FIRST["ff", l], SEQ, GROUPS_2, 1)
                stage_end()
                layer_norm(("ln3", l))
            for i in range(8):
                for k in range(4):
                    m = pe.transpose(PS[:, i, k * P:(k + 1) * P], XT[:, 4 * (i % 2) + k, i // 2 * P:(i // 2 + 1) * P],
                                     IDENT)
                m.then_inc(*mark("out_turned", i))

        @block.scalar
        def _(act):
            stage = [0]

            def stage_end():
                stage[0] += 1
                act.drain().then_inc(*mark("stage_end", ("act", stage[0])))
                act.wait_ge(sems["stage_end"], 3 * stage[0])

            def split(c):
                nk = CHUNKS[c][3]
                act.wait_ge(*at(f"w_loaded{c % NRAW}", c))
                if c >= NSPLIT:
                    act.wait_ge(*at("w_used", c - NSPLIT))
                nc.scalar.activation(WH[:, c % NSPLIT, 0:nk, :], RAW[:, c % NRAW, 0:nk, :], ACT.Copy).then_inc(
                    *mark("w_hi", c))

            def split_ahead(c):
                if c + AHEAD < len(CHUNKS):
                    split(c + AHEAD)

            def rows_in():
                act.wait_ge(*at("zeroed", "rows"))
                views = {"b_ada": A["b_ada"].rearrange("l (r p) -> (l r) p", p=P),
                         "conv_w": A["conv_w"].rearrange("l t (r p) -> (l t r) p", p=P),
                         "conv_b": A["conv_b"].rearrange("l (r p) -> (l r) p", p=P),
                         "conv_w_2": A["conv_w_2"].rearrange("l t (r p) -> (l t r) p", p=P),
                         "c": A["c"].rearrange("b (r p) -> (b r) p", p=P),
                         "c_ctx": A["c_ctx"].rearrange("(r p) -> r p", p=P)}
                for name, (c0, n) in PCOL.items():
                    if name == "gains":
                        continue
                    v = views[name] if name in views else A[name].rearrange("l (r p) -> (l r) p", p=P)
                    a = c0
                    while a < c0 + n:
                        b = min(c0 + n, (a // P + 1) * P)
                        act.dma_start(PROWS[a % P:a % P + b - a, a // P, :], v[a - c0:b - c0, :]).then_inc(
                            *mark("rows_in", (name, a), 16))
                        a = b
                for l in range(DEPTH):
                    for i, name in enumerate(GAINS):
                        c = PCOL["gains"][0] + l * 6 + i
                        w = A[name].shape[1]
                        for r in range(P // w):
                            act.dma_start(PROWS[c % P:c % P + 1, c // P, r * w:(r + 1) * w], A[name][l:l + 1, :]).then_inc(
                                *mark("rows_in", "last" if (l, i, r) == (DEPTH - 1, 5, P // w - 1) else (name, l, r), 16))
                act.dma_start(RPBR[:, 48:79], A["rpb_b"].rearrange("l h a b -> (l h a) b")).then_inc(
                    *mark("bias_in", "rpb", 16))
                act.dma_start(RELR[:, 127:127 + REL_SIZE], A["rel_reversed"].rearrange("l h r -> (l h) r")).then_inc(
                    *mark("bias_in", "last", 16))

            def norm(S, src, T, bias):
                for k in range(KT):
                    if k >= 2:
                        act.wait_ge(*at("sum_step", (S, max(k - 2, 1))))
                    nc.scalar.activation(SQ[k % 2][:, 0:T], src[:, k, 0:T], ACT.Square).then_inc(
                        *mark("sq_ready", (S, k)))
                act.wait_ge(*at("stat_done", S))
                nc.scalar.activation(RSTD[:, 0:T], PS[:, 0, 0:T], ACT.Sqrt, bias=EPSC[:, 0:1]).then_inc(
                    *mark("std_ready", S))
                for k in range(KT):
                    act.wait_ge(*at("norm_mid", (S, k)))
                    nc.scalar.activation(HH[:, k, 0:T], TMP[k % 2][:, 0:T], ACT.Identity, bias=bias(k)).then_inc(
                        *mark("h_hi", (S, k)))
                stage_end()

            def project(S, tiles, c0, T, dst, off):
                n = len(tiles)
                for i in range(n + 1):
                    if i < n:
                        split_ahead(c0 + i)
                        t = tiles[i]
                        ps = PS[:, lin_bank(i), 0:T]
                        act.wait_ge(*at("w_used", c0 + i))
                        if "blk" in t or is_value(t):
                            p = aux_before(tiles, i)
                            if p is not None:
                                act.wait_ge(*at("v_turned" if is_value(tiles[p]) else "blk_done", (S, p)))
                        if "blk" in t:
                            nc.scalar.activation(SQ[i % 2][:, 0:T], ps, ACT.Square).then_inc(
                                *mark("raw_squared", (S, i)))
                        to = SQ[i % 2][:, 0:T] if is_value(t) else dst[:, t["slot"], off:off + T]
                        nc.scalar.activation(to, ps, ACT.Copy, scale=t.get("scale", 1.0)).then_inc(
                            *mark("raw_copied", (S, i)))
                    j = i - 1
                    if 0 <= j < n and "blk" in tiles[j]:
                        act.wait_ge(*at("blk_done", (S, j)))
                        if j >= 2 and "blk" in tiles[j - 2]:
                            act.wait_ge(*at("qk_step", (S, j - 2, "norm")))
                        nc.scalar.activation(TMP[j % 2][:, 0:T], PS[:, 4 + j % 2, 0:T], ACT.Sqrt,
                                             bias=EPSC[:, 0:1], scale=1.0 / (64, 32)[tiles[j]["blk"]]).then_inc(
                                                 *mark("blk_std", (S, j)))

            def out_proj(c0):
                for n in range(KT):
                    split_ahead(c0 + n)

            def attend(att):
                S, units, groups, PTt = att["S"], att["units"], att["groups"], att["PT"]
                owner = {s: u for u, unit in enumerate(units) for s in unit["sub"]}
                for i in range(len(units) + 5):
                    if i < len(units):
                        u = units[i]
                        for m, s in enumerate(u["sub"]):
                            act.wait_ge(*at("neg_max", (S, s)))
                            if s >= 3:
                                o = owner[s - 3]
                                act.wait_ge(*at("probs_turned_b" if units[o]["nk"] > 512 else "probs_turned_a", (S, o)))
                            if u["head"] == 0 and u["group"] >= 2:
                                act.wait_ge(*at("o_step", (S, u["group"] - 2, "scaled")))
                            nc.scalar.activation(
                                PROB[s % 3][:, 0:u["nk"]],
                                PS[:, 2 * (s % 2):2 * (s % 2) + 2, :].rearrange("p b c -> p (b c)")[:, 0:u["nk"]],
                                ACT.Exp, bias=NMAX[:, s % 4:s % 4 + 1],
                                accum_out=SUMS[:, u["group"] % 2, 8 * m + u["head"]:8 * m + u["head"] + 1]).then_inc(
                                    *mark("exp_done", (S, s)))
                    j = i - 1
                    if 0 <= j < len(units):
                        u = units[j]
                        w = min(u["nk"], 512)
                        act.wait_ge(*at("probs_turned_a", (S, j)))
                        if j >= 2:
                            act.wait_ge(*at("pv_done", (S, j - 2)))
                        nc.scalar.activation(PTt[:, j % 2, 0:w], PS[:, 4, 0:w], ACT.Copy).then_inc(
                            *mark("pt_copied_a", (S, j)))
                    j = i - 3
                    if 0 <= j < len(units) and units[j]["last"] and groups[units[j]["group"]]["diff"]:
                        g = units[j]["group"]
                        act.wait_ge(*at("o_step", (S, g, "ss")))
                        nc.scalar.activation(SSQ[:, 1, :], SSQ[:, 0, :], ACT.Sqrt, bias=EPSC[:, 0:1],
                                             scale=1.0 / HEAD).then_inc(*mark("sub_std", (S, g)))
                    j = i - 4
                    if 0 <= j < len(units) and units[j].get("tile_last"):
                        t, f = units[j]["t"], att["first"]
                        for part, bank, a, b in (("a", 4, 0, 4), ("b", 5, 4, att["tiles"])):
                            act.wait_ge(*at(f"o_turned_{part}", (S, t)))
                            nc.scalar.activation(HH[:, f + a:f + b, t * P:(t + 1) * P],
                                                 PS[:, bank, 0:(b - a) * P].rearrange("p (k c) -> p k c", c=P),
                                                 ACT.Copy).then_inc(*mark("o_hi", (S, t, part)))

            def ffn(S, c0, T, l, groups, parts):
                total = sum(n for _, n in groups)
                place = [(g, j) for g, (_, n) in enumerate(groups) for j in range(n)]
                downs = {}
                steps = ffn_steps(groups, parts)
                for n, step in enumerate(steps):
                    if step[0] == "down":
                        downs[step[1]] = c0 + n

                def silu(q):
                    act.wait_ge(*at("conv_step", (S, 2 * q + 1, "after")))
                    nc.scalar.activation(MG[:, q % 3, 0:T], MG[:, q % 3, 0:T], ACT.Silu).then_inc(
                        *mark("silu_ready", (S, q)))

                def hidden_hi(q):
                    g, j = place[q]
                    act.wait_ge(*at("prod_ready", (S, q)))
                    if g >= 2 and j == 0:
                        act.wait_ge(*at("w_used", downs[g - 2]))
                    nc.scalar.activation(GH[:, g % 2, j, 0:T], MG[:, q % 3, 0:T], ACT.Copy).then_inc(
                        *mark("hid_hi", (S, q)))

                up = 0
                for n, step in enumerate(steps):
                    split_ahead(c0 + n)
                    if step[0] == "down":
                        continue
                    q, part = up // parts, up % parts
                    act.wait_ge(*at("w_used", c0 + n))
                    if q >= 3:
                        act.wait_ge(*at("hid_lo", (S, q - 3)))
                    if parts == 2:
                        i = part * FT + q
                        nc.scalar.activation((MU, MG)[part][:, q % 3, 0:T], PS[:, lin_bank(up), 0:T], ACT.Identity,
                                             bias=prm("conv_b", l * 2 * FT + i),
                                             scale=prm("conv_w", l * 6 * FT + 2 * FT + i)).then_inc(
                                                 *mark("mid_ready", (S, up)))
                        if part == 1:
                            if q >= 1:
                                silu(q - 1)
                            if q >= 2:
                                hidden_hi(q - 2)
                            if q == total - 1:
                                silu(q)
                                hidden_hi(q - 1)
                                hidden_hi(q)
                    else:
                        nc.scalar.activation(MU[:, q % 3, 0:T], PS[:, lin_bank(up), 0:T], ACT.Relu).then_inc(
                            *mark("mid_ready", (S, up)))
                        if q >= 1:
                            hidden_hi(q - 1)
                        if q == total - 1:
                            hidden_hi(q)
                    up += 1

            def layer_norm(S, mem=None):
                if mem is not None:
                    nc.scalar.activation(MH[:, :, :], CT[:, :, :], ACT.Copy).then_inc(*mark("mem_hi_made", mem))
                for k in range(KT):
                    act.wait_ge(*at("norm_step", (S, k)))
                    if k >= 2:
                        act.wait_ge(*at("sum_step", ((S, "var"), max(k - 2, 1))))
                    nc.scalar.activation(SQ[k % 2], XT[:, k, :], ACT.Square).then_inc(*mark("sq_ready", (S, k)))
                act.wait_ge(*at("stat_done", (S, "var")))
                nc.scalar.activation(RSTD[:, :], PS[:, 1, :], ACT.Sqrt, bias=EPSC[:, 1:2]).then_inc(
                    *mark("std_ready", S))
                name = S[0]
                for k in range(KT):
                    act.wait_ge(*at("norm_mid", (S, k)))
                    nc.scalar.activation(XT[:, k, :], TMP[k % 2], ACT.Identity,
                                         bias=prm(name + "_b_2", S[1] * KT + k)).then_inc(*mark("x_ready", (S, k)))
                    act.wait_ge(*at("x_ready", (S, k)))
                    nc.scalar.activation(HH[:, k, :], XT[:, k, :], ACT.Copy).then_inc(*mark("h_hi", (S, k)))
                stage_end()

            act.dma_start(PACK[:, :], A["const_pack"]).then_inc(*mark("consts_in", "pack", 16))
            for i, name in enumerate(("lambda_q1", "lambda_k1", "lambda_q2", "lambda_k2")):
                for l in range(DEPTH):
                    act.dma_start(LAMV[:, l, i, :], A[name][l:l + 1, :].broadcast_to([P, 32])).then_inc(
                        *mark("consts_in", (name, l), 16))
            for l in range(DEPTH):
                act.dma_start(GSUB[:, l, :], A["g_subln"][l:l + 1, :].broadcast_to([P, HEAD])).then_inc(
                    *mark("consts_in", ("g_sub", l), 16))
            act.dma_start(RELC[:, :], bass.AP(A["rel_reversed"].tensor, 0, [[0, P], [REL_SIZE, 12]]),
                          allow_slow_non_contiguous=True).then_inc(*mark("consts_in", "last", 16))
            rows_in()
            for i in range(6):
                src = A["x"][0, i * P:(i + 1) * P, :] if i < 4 else A["ctx"][0, (i - 4) * P:(i - 3) * P, :]
                act.dma_start(XN[:, i, :], src).then_inc(*mark("acts_in", "last" if i == 5 else i, 16))
            act.wait_ge(*at("zeroed", "rel"))
            act.dma_start(RPB_PAD, RPBR[:, :].unsqueeze(1).broadcast_to([120, 64, P])).then_inc(
                *mark("pad_written", "rpb", 16))
            act.dma_start(REL_PAD, RELR[:, :].unsqueeze(1).broadcast_to([12, P, 384])).then_inc(
                *mark("pad_written", "last", 16))
            act.wait_ge(*at("turned_taken", "params"))
            c0 = PCOL["c"][0] % P
            silu_in = PRM[:, PCOL["c"][0] // P, c0:c0 + 16].rearrange("p (s k) -> p k s", s=2)
            nc.scalar.activation(SILU[:, :, :], silu_in, ACT.Silu).then_inc(*mark("param_act", "silu"))
            act.wait_ge(*at("param_step", "lam_sum"))
            nc.scalar.activation(LAM[:, :, 0:2], LAM[:, :, 2:4], ACT.Exp).then_inc(*mark("param_act", "lam_exp"))
            act.wait_ge(*at("pad_written", "last"))
            stage_end()
            for c in range(AHEAD):
                split(FIRST["qkv", "c", 0] + c)
            stage_end()
            for l in range(DEPTH):
                for i in range(4):
                    act.dma_start(ROPE[:, i, :], A["const_rope"][:, i, :]).then_inc(
                        *mark("tab_in", ("rope", l) if i == 3 else (l, i), 16))
                for part in range(2):
                    for h in range(B_HEADS):
                        row = (l * B_HEADS + h) * 15 + 1 - part
                        act.dma_start(TB[64 * part:64 * part + 64, h, :, :],
                                      bass.AP(RPB_PAD.tensor, row * 64 * P + 63, [[P - 1, 64], [64 * P, 14], [1, 64]])
                                      ).then_inc(*mark("tab_in", ("win", l) if (part, h) == (1, 3) else (l, part, "w", h), 16))
                for s in ("c", "x"):
                    norm(("n1", s, l), XT if s == "x" else CT, TOKENS[s],
                         lambda k: MOD[:, l, k, int(s == "c"):int(s == "c") + 1])
                    project(("qkv", s, l), qkv_tiles(s, l), FIRST["qkv", s, l], TOKENS[s], QK, SEQ if s == "c" else 0)
                    stage_end()
                for s in streams(l):
                    attend(number_attention(("att", s, l), attention_units_1(s, l)))
                    stage_end()
                    out_proj(FIRST["out", s, l])
                    stage_end()
                for s in streams(l):
                    norm(("n2", s, l), XT if s == "x" else CT, TOKENS[s],
                         lambda k: MOD[:, l, 24 + k, int(s == "c"):int(s == "c") + 1])
                    ffn(("ffn", s, l), FIRST["ffn", s, l], TOKENS[s], l, GROUPS_1, 2)
                    stage_end()
            for i in range(2):
                act.dma_start(XN[:, i, :], A["mem_2"][0, i * P:(i + 1) * P, :]).then_inc(
                    *mark("mem_in", "last" if i else 0, 16))
            for k in range(KT):
                nc.scalar.activation(HH[:, k, :], XT[:, k, :], ACT.Copy).then_inc(*mark("h_hi", ("x", k)))
            stage_end()
            for l in range(DEPTH):
                act.dma_start(POSI[:, :], A["positions_2"][0:1, :].broadcast_to([P, SEQ])).then_inc(
                    *mark("tab_in", ("pos", l), 16))
                for h in range(6):
                    act.dma_start(TBK[:, h, :], bass.AP(REL_PAD.tensor, (l * 6 + h) * P * 384 + 127, [[383, P], [1, 256]])
                                  ).then_inc(*mark("bias2_in", (l, h), 16))
                for i in range(4):
                    act.wait_ge(*at("trig_step", (l, i, "max")))
                    nc.scalar.activation(ROPE2[:, i, :], ROPE2[:, i, :], ACT.Sin).then_inc(*mark("trig_act", (l, i)))
                project(("mix_in", l), mixer_tiles(), FIRST["mix_in", l], SEQ, QK2, 0)
                stage_end()
                for m in range(2):
                    act.wait_ge(*at("cv_step", (l, m, "y")))
                    nc.scalar.activation(HH[:, m, :], TMP[m], ACT.Copy).then_inc(*mark("cv_hi", (l, m)))
                for n, (t, h) in enumerate(INDEX_STEPS):
                    act.wait_ge(*at("idx_done", (l, n)))
                    if n >= 2:
                        act.wait_ge(*at("idx_step", (l, n - 2)))
                    nc.scalar.activation(SQ[n % 2][:, 0:(t + 1) * P], PS[:, n % 2, 0:(t + 1) * P], ACT.Relu).then_inc(
                        *mark("idx_relu", (l, n)))
                stage_end()
                attend(number_attention(("att2", l), attention_units_2(l)))
                stage_end()
                out_proj(FIRST["mix_out", l])
                stage_end()
                layer_norm(("ln1", l), mem=l)
                kv = ("mem_kv", l)
                for n in range(2 * KT):
                    split_ahead(FIRST[kv] + n)
                    act.wait_ge(*at("w_used", FIRST[kv] + n))
                    if n >= KT + 2:
                        act.wait_ge(*at("v_turned", (kv, n - 2)))
                    nc.scalar.activation(MK[:, n, :] if n < KT else SQ[n % 2][:, 0:MEM], PS[:, lin_bank(n), 0:MEM],
                                         ACT.Copy).then_inc(*mark("raw_copied", (kv, n)))
                for n in range(KT):
                    split_ahead(FIRST["mem_q", l] + n)
                    act.wait_ge(*at("w_used", FIRST["mem_q", l] + n))
                    nc.scalar.activation(MQ[:, n, :], PS[:, lin_bank(n), :], ACT.Copy, scale=1.0 / 16).then_inc(
                        *mark("raw_copied", (("mem_q", l), n)))
                stage_end()
                attend(number_attention(("att3", l), attention_units_3()))
                stage_end()
                out_proj(FIRST["mem_out", l])
                stage_end()
                layer_norm(("ln2", l))
                ffn(("ff", l), FIRST["ff", l], SEQ, l, GROUPS_2, 1)
                stage_end()
                layer_norm(("ln3", l))
            for i in range(8):
                act.wait_ge(*at("out_turned", i))
                nc.scalar.activation(OUTS[:, i // 2, 512 * (i % 2):512 * (i % 2) + 512], PS[:, i, :], ACT.Copy).then_inc(
                    *mark("out_copied", i))
                if i % 2:
                    act.wait_ge(*at("out_copied", i))
                    act.dma_start(out[0, i // 2 * P:(i // 2 + 1) * P, :], OUTS[:, i // 2, :]).then_inc(
                        *mark("out_stored", i, 16))
            act.wait_ge(*at("out_stored", 7))

        @block.vector
        def _(dve):
            stage = [0]

            def stage_end():
                stage[0] += 1
                dve.drain().then_inc(*mark("stage_end", ("dve", stage[0])))
                dve.wait_ge(sems["stage_end"], 3 * stage[0])

            def own(name, key, ins):
                ins.then_inc(*mark(name, key))
                dve.wait_ge(*at(name, key))

            def lo(name, key, out_ap, full, hi):
                nc.vector.tensor_tensor(out_ap, full, hi.bitcast(F32), ALU.subtract).then_inc(*mark(name, key))

            def add_up(S, tile, wait, T):
                for k in range(1, KT):
                    for m in ((0, 1) if k == 1 else (k,)):
                        wait(m)
                    a = tile(0) if k == 1 else ACC[:, 0:T]
                    nc.vector.tensor_tensor(ACC[:, 0:T], a, tile(k), ALU.add).then_inc(
                        *mark("sum_step", (S, "total" if k == KT - 1 else k)))
                    dve.wait_ge(*at("sum_step", (S, "total" if k == KT - 1 else k)))

            def turn_in(S, n, dst):
                for i in range(n):
                    for half in range(2):
                        dve.wait_ge(*at("turned", (S, 2 * i + half)))
                        d, t = dst(i)
                        nc.vector.tensor_copy(d[:, 4 * half:4 * half + 4, t * P:(t + 1) * P],
                                              PS[:, (2 * i + half) % 8, :].rearrange("p (k c) -> p k c", c=P)).then_inc(
                                                  *mark("turned_taken", (S, 2 * i + half)))

            def norm(S, src, T, gain, bias):
                add_up(S, lambda k: SQ[k % 2][:, 0:T], lambda k: dve.wait_ge(*at("sq_ready", (S, k))), T)
                dve.wait_ge(*at("std_ready", S))
                own("norm_step", (S, "recip"), nc.vector.reciprocal(RSTD[:, 0:T], RSTD[:, 0:T]))
                for k in range(KT + 1):
                    if k < KT:
                        if k >= 2:
                            dve.wait_ge(*at("h_lo", (S, k - 2)))
                        nc.vector.scalar_tensor_tensor(TMP[k % 2][:, 0:T], src[:, k, 0:T], gain(k), RSTD[:, 0:T],
                                                       ALU.mult, ALU.mult).then_inc(*mark("norm_mid", (S, k)))
                    if k:
                        j = k - 1
                        dve.wait_ge(*at("h_hi", (S, j)))
                        nc.vector.scalar_tensor_tensor(HL[:, j, 0:T], TMP[j % 2][:, 0:T], bias(j),
                                                       HH[:, j, 0:T].bitcast(F32), ALU.add, ALU.subtract).then_inc(
                                                           *mark("h_lo", (S, j)))
                stage_end()

            def project(S, tiles, c0, T, dst, off, tables, v_dst):
                n = len(tiles)
                rotated = []
                for i in range(n + 2):
                    j = i - 1
                    if 0 <= j < n and "blk" in tiles[j]:
                        t = tiles[j]
                        q = dst[:, t["slot"], off:off + T]
                        r = TMP[j % 2][:, 0:T]
                        dve.wait_ge(*at("blk_std", (S, j)))
                        own("qk_step", (S, j, "recip"), nc.vector.reciprocal(r, r))
                        dve.wait_ge(*at("raw_copied", (S, j)))
                        nc.vector.scalar_tensor_tensor(q, q, HG[:, S[2], t["gain"]:t["gain"] + 1], r, ALU.mult,
                                                       ALU.mult).then_inc(*mark("qk_step", (S, j, "norm")))
                    j = i - 2
                    if 0 <= j < n and tiles[j]["kind"] == "qk" and tiles[j]["rope"] is not None:
                        t = tiles[j]
                        q = dst[:, t["slot"], off:off + T]
                        r = (ACC, RSTD)[j % 2][:, 0:T]
                        dve.wait_ge(*at("rot_done", (S, j)))
                        prev = [m for m in rotated if m % 2 == j % 2]
                        if prev:
                            dve.wait_ge(*at("rope_step", (S, prev[-1], "sum")))
                        rotated.append(j)
                        nc.vector.tensor_tensor(r, PS[:, 6 + j % 2, 0:T], tables[:, t["rope"] + 1, 0:T], ALU.mult).then_inc(
                            *mark("rope_step", (S, j, "sin")))
                        own("rope_step", (S, j, "cos"), nc.vector.tensor_tensor(q, q, tables[:, t["rope"], 0:T], ALU.mult))
                        nc.vector.tensor_tensor(q, q, r, ALU.add).then_inc(*mark("rope_step", (S, j, "sum")))
                    j = i - 1
                    if 0 <= j < n and is_value(tiles[j]):
                        dve.wait_ge(*at("v_turned", (S, j)))
                        nc.vector.tensor_copy(v_dst(tiles[j]), PS[:, 4 + j % 2, 0:T].rearrange("p (t c) -> p t c", c=P)
                                              ).then_inc(*mark("v_copied", (S, j)))

            def residual(S, n, c, ps, k, T, x, gate, scale, prev=None):
                dve.wait_ge(*at("w_used", c))
                if prev is not None:
                    dve.wait_ge(*at("resid", prev))
                if gate is not None:
                    i = nc.vector.scalar_tensor_tensor(x[:, k, 0:T], ps, gate, x[:, k, 0:T], ALU.mult, ALU.add)
                else:
                    i = nc.vector.scalar_tensor_tensor(x[:, k, 0:T], x[:, k, 0:T], scale, ps, ALU.mult, ALU.add)
                i.then_inc(*mark("resid", (S, n)))

            def out_proj(S, c0, T, x, gate):
                for n in range(KT):
                    residual(S, n, c0 + n, PS[:, lin_bank(n), 0:T], n, T, x, gate(n), ALPHA)

            def attend(att):
                S, units, groups, PTt, ONt = att["S"], att["units"], att["groups"], att["PT"], att["ON"]
                for i in range(len(units) + 5):
                    if i < len(units):
                        u = units[i]
                        for s in u["sub"]:
                            ps = PS[:, 2 * (s % 2):2 * (s % 2) + 2, :].rearrange("p b c -> p (b c)")
                            dve.wait_ge(*at("scores_done", (S, s)))
                            for n, (a, b, bias) in enumerate(u["adds"]):
                                if bias.shape[1] == 1:
                                    ins = nc.vector.tensor_scalar(ps[:, a:b], ps[:, a:b], bias, None, ALU.add)
                                else:
                                    ins = nc.vector.tensor_tensor(ps[:, a:b], ps[:, a:b], bias, ALU.add)
                                own("bias_step", (S, s, n), ins)
                            nc.vector.tensor_reduce(NMAX[:, s % 4:s % 4 + 1], ps[:, 0:u["nk"]], AX.X, ALU.max,
                                                    negate=True).then_inc(*mark("neg_max", (S, s)))
                    j = i - 1
                    if 0 <= j < len(units):
                        u = units[j]
                        g, h, nk = u["group"], u["head"], u["nk"]
                        if len(u["sub"]) == 2:
                            s0, s1 = u["sub"]
                            dve.wait_ge(*at("exp_done", (S, s1)))
                            own("mix_step", (S, j, "recip"),
                                nc.vector.reciprocal(COEF[:, 0:1], SUMS[:, g % 2, 8 + h:9 + h]))
                            own("mix_step", (S, j, "coef"),
                                nc.vector.tensor_scalar(COEF[:, 1:2], SUMS[:, g % 2, h:h + 1], COEF[:, 0:1],
                                                        LAM[:, groups[g]["layer"], 2:3], ALU.mult, ALU.mult))
                            own("mix_step", (S, j, "mixed"),
                                nc.vector.scalar_tensor_tensor(PROB[s0 % 3][:, 0:nk], PROB[s1 % 3][:, 0:nk], COEF[:, 1:2],
                                                               PROB[s0 % 3][:, 0:nk], ALU.mult, ALU.add))
                        if nk > 512:
                            dve.wait_ge(*at("probs_turned_b", (S, j)))
                            if j >= 2:
                                dve.wait_ge(*at("pv_done", (S, j - 2)))
                            nc.vector.tensor_copy(PTt[:, j % 2, 512:nk], PS[:, 5, 0:nk - 512]).then_inc(
                                *mark("pt_copied_b", (S, j)))
                    j = i - 3
                    if 0 <= j < len(units) and units[j]["last"]:
                        u = units[j]
                        g, t = u["group"], u["t"]
                        gr = groups[g]
                        nh, dv = gr["heads"], gr["dv"]
                        on = ONt[:, t % 2, gr["col"]:gr["col"] + nh * dv].rearrange("p (h d) -> p h d", d=dv)
                        dve.wait_ge(*at("pv_done", (S, j)))
                        if t >= 2:
                            dve.wait_ge(*at("o_turned_b", (S, t - 2)))
                        own("o_step", (S, g, "recip"), nc.vector.reciprocal(RSUM[:, g % 2, 0:nh], SUMS[:, g % 2, 0:nh]))
                        own("o_step", (S, g, "scaled"),
                            nc.vector.tensor_tensor(on, PS[:, 6 + g % 2, 0:nh * dv].rearrange("p (h d) -> p h d", d=dv),
                                                    RSUM[:, g % 2, 0:nh].unsqueeze(2).broadcast_to([P, nh, dv]), ALU.mult))
                        if gr["diff"]:
                            sq = ACC[:, 0:nh * dv].rearrange("p (h d) -> p h d", d=dv)
                            own("o_step", (S, g, "sq"), nc.vector.tensor_tensor(sq, on, on, ALU.mult))
                            nc.vector.tensor_reduce(SSQ[:, 0, :], sq, AX.X, ALU.add).then_inc(
                                *mark("o_step", (S, g, "ss")))
                    j = i - 4
                    if 0 <= j < len(units) and units[j]["last"] and groups[units[j]["group"]]["diff"]:
                        u = units[j]
                        g, t = u["group"], u["t"]
                        gr = groups[g]
                        nh, dv = gr["heads"], gr["dv"]
                        on = ONt[:, t % 2, gr["col"]:gr["col"] + nh * dv].rearrange("p (h d) -> p h d", d=dv)
                        dve.wait_ge(*at("sub_std", (S, g)))
                        own("o_step", (S, g, "rstd"), nc.vector.reciprocal(SSQ[:, 1, :], SSQ[:, 1, :]))
                        own("o_step", (S, g, "normed"),
                            nc.vector.tensor_tensor(on, on, SSQ[:, 1, :].unsqueeze(2).broadcast_to([P, nh, dv]), ALU.mult))
                        nc.vector.tensor_tensor(on, on, GSUB[:, gr["layer"], :].unsqueeze(1).broadcast_to([P, nh, dv]),
                                                ALU.mult).then_inc(*mark("o_step", (S, g, "ready")))
                    if 0 <= j < len(units) and units[j].get("tile_last"):
                        t, f = units[j]["t"], att["first"]
                        for part, bank, a, b in (("a", 4, 0, 4), ("b", 5, 4, att["tiles"])):
                            dve.wait_ge(*at("o_hi", (S, t, part)))
                            lo("o_lo", (S, t, part), HL[:, f + a:f + b, t * P:(t + 1) * P],
                               PS[:, bank, 0:(b - a) * P].rearrange("p (k c) -> p k c", c=P),
                               HH[:, f + a:f + b, t * P:(t + 1) * P])

            def ffn(S, c0, T, l, groups, parts, x, gate):
                total = sum(n for _, n in groups)
                place = [(g, j) for g, (_, n) in enumerate(groups) for j in range(n)]

                def product(q):
                    if parts == 2:
                        dve.wait_ge(*at("silu_ready", (S, q)))
                        nc.vector.tensor_tensor(MG[:, q % 3, 0:T], MG[:, q % 3, 0:T], MU[:, q % 3, 0:T],
                                                ALU.mult).then_inc(*mark("prod_ready", (S, q)))
                    else:
                        dve.wait_ge(*at("mid_ready", (S, q)))
                        if q >= 3:
                            dve.wait_ge(*at("hid_lo", (S, q - 3)))
                        nc.vector.tensor_tensor(MG[:, q % 3, 0:T], MU[:, q % 3, 0:T], MU[:, q % 3, 0:T],
                                                ALU.mult).then_inc(*mark("prod_ready", (S, q)))

                def hidden_lo(q):
                    g, j = place[q]
                    dve.wait_ge(*at("hid_hi", (S, q)))
                    lo("hid_lo", (S, q), GL[:, g % 2, j, 0:T], MG[:, q % 3, 0:T], GH[:, g % 2, j, 0:T])

                up = down = 0
                for n, step in enumerate(ffn_steps(groups, parts)):
                    if step[0] == "down":
                        _, g, k = step
                        residual(S, down, c0 + n, PS[:, 4 + down % 4, 0:T], k, T, x, gate(k), ALPHA if g == 0 else 1.0,
                                 (S, down - KT) if down >= KT else None)
                        down += 1
                        continue
                    q, part = up // parts, up % parts
                    if parts == 2:
                        i = l * 6 * FT + part * FT + q
                        m = (MU, MG)[part]
                        ps = PS[:, lin_bank(up), 0:T]
                        dve.wait_ge(*at("mid_ready", (S, up)))
                        own("conv_step", (S, up, "before"), nc.vector.scalar_tensor_tensor(
                            m[:, q % 3, 1:T], ps[:, 0:T - 1], prm("conv_w", i), m[:, q % 3, 1:T], ALU.mult, ALU.add))
                        nc.vector.scalar_tensor_tensor(
                            m[:, q % 3, 0:T - 1], ps[:, 1:T], prm("conv_w", i + 4 * FT), m[:, q % 3, 0:T - 1],
                            ALU.mult, ALU.add).then_inc(*mark("conv_step", (S, up, "after")))
                        if part == 1:
                            if q >= 1:
                                product(q - 1)
                            if q >= 2:
                                hidden_lo(q - 2)
                            if q == total - 1:
                                product(q)
                                hidden_lo(q - 1)
                                hidden_lo(q)
                    else:
                        product(q)
                        if q >= 1:
                            hidden_lo(q - 1)
                        if q == total - 1:
                            hidden_lo(q)
                    up += 1

            def layer_norm(S, mem=None):
                if mem is not None:
                    dve.wait_ge(*at("mem_hi_made", mem))
                    lo("mem_lo_made", mem, ML[:, :, :], CT[:, :, :], MH[:, :, :])
                add_up((S, "mean"), lambda k: XT[:, k, :], lambda k: None, SEQ)
                dve.wait_ge(*at("stat_done", (S, "mean")))
                for k in range(KT):
                    nc.vector.tensor_tensor(XT[:, k, :], XT[:, k, :], PS[:, 0, :], ALU.subtract).then_inc(
                        *mark("norm_step", (S, k)))
                add_up((S, "var"), lambda k: SQ[k % 2], lambda k: dve.wait_ge(*at("sq_ready", (S, k))), SEQ)
                dve.wait_ge(*at("std_ready", S))
                own("norm_step", (S, "recip"), nc.vector.reciprocal(RSTD[:, :], RSTD[:, :]))
                for k in range(KT + 1):
                    if k < KT:
                        if k >= 2:
                            dve.wait_ge(*at("x_ready", (S, k - 2)))
                        nc.vector.scalar_tensor_tensor(TMP[k % 2], XT[:, k, :], prm(S[0] + "_g_2", S[1] * KT + k),
                                                       RSTD[:, :], ALU.mult, ALU.mult).then_inc(*mark("norm_mid", (S, k)))
                    if k:
                        dve.wait_ge(*at("h_hi", (S, k - 1)))
                        lo("h_lo", (S, k - 1), HL[:, k - 1, :], XT[:, k - 1, :], HH[:, k - 1, :])
                stage_end()

            nc.vector.memset(PROWS[:, NGRP - 1, :], 0.0).then_inc(*mark("zeroed", "prows"))
            nc.vector.memset(RPBR[:, :], 0.0).then_inc(*mark("zeroed", "rpb"))
            nc.vector.memset(RELR[:, :], 0.0).then_inc(*mark("zeroed", "rows"))
            nc.vector.memset(EPSC[:, 0:1], EPS).then_inc(*mark("zeroed", "eps"))
            nc.vector.memset(EPSC[:, 1:2], LN_EPS).then_inc(*mark("zeroed", "ln_eps"))
            dve.wait_ge(*at("bias_in", "last"))
            nc.vector.tensor_scalar(RELR[:, 0:127], RELR[:, 0:127], RELR[:, 127:128], None, ALU.add).then_inc(
                *mark("zeroed", "rel"))
            dve.wait_ge(*at("turned", "params"))
            nc.vector.tensor_copy(PRM[:, 0:4, :], PS[:, 6, :].rearrange("p (g c) -> p g c", c=P)).then_inc(
                *mark("param_step", "prm"))
            nc.vector.tensor_copy(PRM[:, 4:NGRP, :], PS[:, 7, 0:(NGRP - 4) * P].rearrange("p (g c) -> p g c", c=P)).then_inc(
                *mark("turned_taken", "params"))
            dve.wait_ge(*at("turned_taken", "params"))
            dve.wait_ge(*at("param_step", "prm"))
            for i, scale in enumerate((0.125, 1.0, 0.125, 1.0, 32.0 ** -0.5, 1.0)):
                src = prm_range("gains", 0, 12).rearrange("p (l i) -> p l i", i=6)[:, :, i]
                nc.vector.tensor_scalar(HG[:, :, i], src, scale, None, ALU.mult).then_inc(*mark("param_step", ("hg", i)))
            prod = ACC[:, 0:128].rearrange("p (l a d) -> p l a d", l=2, a=2)
            for l in range(DEPTH):
                v = LAMV[:, l, :, :].rearrange("p (a b) d -> p a b d", b=2)
                own("param_step", ("lam_prod", l), nc.vector.tensor_tensor(prod[:, l], v[:, :, 0, :], v[:, :, 1, :], ALU.mult))
                nc.vector.tensor_reduce(LAM[:, l, 2:4], prod[:, l], AX.X, ALU.add).then_inc(
                    *mark("param_step", "lam_sum" if l else ("lam_sum", l)))
            dve.wait_ge(*at("param_act", "lam_exp"))
            for l in range(DEPTH):
                lam_init = 0.8 - 0.6 * math.exp(-0.3 * l)
                own("param_step", ("lam_diff", l), nc.vector.tensor_tensor(LAM[:, l, 3:4], LAM[:, l, 1:2], LAM[:, l, 0:1],
                                                                          ALU.subtract))
                own("param_step", ("neg_lam", l), nc.vector.tensor_scalar(LAM[:, l, 2:3], LAM[:, l, 3:4], -lam_init, None,
                                                                         ALU.add))
                nc.vector.tensor_scalar(GSUB[:, l, :], GSUB[:, l, :], 1.0 - lam_init, None, ALU.mult).then_inc(
                    *mark("param_step", ("g_sub", l)))
            turn_in("in", 6, lambda i: (XT, i) if i < 4 else (CT, i - 4))
            stage_end()
            for b in range(24):
                dve.wait_ge(*at("w_used", FIRST["ada", 0] + 4 * b + 3))
                nc.vector.tensor_copy(MROW[:, b * 512:(b + 1) * 512], PS[0:2, b % 8, :]).then_inc(*mark("mod_rows", b))
            dve.wait_ge(*at("turned", "mod"))
            for l in range(DEPTH):
                own("param_step", ("mod", l), nc.vector.tensor_tensor(
                    MOD[:, l, :, :], PS[:, l, 0:96].rearrange("p (n s) -> p n s", s=2),
                    prm_range("b_ada", l * 48, 48).unsqueeze(2).broadcast_to([P, 48, 2]), ALU.add))
                for w, name in enumerate(("g_norm1", "g_norm2")):
                    for s in range(2):
                        nc.vector.scalar_tensor_tensor(GMOD[:, l, w, s, :], MOD[:, l, 8 + 24 * w:16 + 24 * w, s], 1.0,
                                                       prm_range(name, l * KT, KT), ALU.add, ALU.mult).then_inc(
                                                           *mark("param_step", ("gmod", l, w, s)))
            stage_end()
            for l in range(DEPTH):
                for s in ("c", "x"):
                    si = int(s == "c")
                    x = CT if si else XT
                    norm(("n1", s, l), x, TOKENS[s], lambda k: GMOD[:, l, 0, si, k:k + 1],
                         lambda k: MOD[:, l, k, si:si + 1])
                    if si:
                        dve.wait_ge(*at("tab_in", ("win", l)))
                        for h in range(B_HEADS):
                            nc.vector.tensor_tensor(TB[:, h], TB[:, h], WINDOW.unsqueeze(1).broadcast_to([P, 14, 64]),
                                                    ALU.add).then_inc(*mark("bias_step", ("window", l, h)))
                    t0 = 4 if si else 0
                    nt = TOKENS[s] // P
                    project(("qkv", s, l), qkv_tiles(s, l), FIRST["qkv", s, l], TOKENS[s], QK, SEQ if si else 0, ROPE,
                            lambda t: VN[:, t0:t0 + nt, t["col"]:t["col"] + P])
                    stage_end()
                for s in streams(l):
                    si = int(s == "c")
                    attend(number_attention(("att", s, l), attention_units_1(s, l)))
                    stage_end()
                    out_proj(("out", s, l), FIRST["out", s, l], TOKENS[s], CT if si else XT,
                             lambda k: MOD[:, l, 16 + k, si:si + 1])
                    stage_end()
                for s in streams(l):
                    si = int(s == "c")
                    x = CT if si else XT
                    norm(("n2", s, l), x, TOKENS[s], lambda k: GMOD[:, l, 1, si, k:k + 1],
                         lambda k: MOD[:, l, 24 + k, si:si + 1])
                    ffn(("ffn", s, l), FIRST["ffn", s, l], TOKENS[s], l, GROUPS_1, 2, x,
                        lambda k: MOD[:, l, 40 + k, si:si + 1])
                    stage_end()
            for k in range(KT):
                dve.wait_ge(*at("h_hi", ("x", k)))
                lo("h_lo", ("x", k), HL[:, k, :], XT[:, k, :], HH[:, k, :])
            turn_in("mem", 2, lambda i: (CT, i))
            stage_end()
            for l in range(DEPTH):
                dve.wait_ge(*at("tab_in", ("pos", l)))
                own("trig_step", (l, "float"), nc.vector.tensor_copy(TMP[0], POSI[:, :]))
                for i in range(4):
                    shift = 0.0 if i % 2 else math.pi / 2
                    r = ROPE2[:, i, :]
                    own("trig_step", (l, i, "angle"), nc.vector.tensor_scalar(SQ[0], TMP[0], FREQ[:, i // 2:i // 2 + 1], None,
                                                                             ALU.mult))
                    own("trig_step", (l, i, "turns"), nc.vector.tensor_scalar(SQ[1], SQ[0], shift, 1.0 / (2 * math.pi),
                                                                             ALU.add, ALU.mult))
                    own("trig_step", (l, i, "round_up"), nc.vector.tensor_scalar(SQ[1], SQ[1], ROUND, None, ALU.add))
                    own("trig_step", (l, i, "round"), nc.vector.tensor_scalar(SQ[1], SQ[1], ROUND, None, ALU.subtract))
                    for n, part in enumerate(TWO_PI_PARTS):
                        own("trig_step", (l, i, n), nc.vector.scalar_tensor_tensor(r, SQ[1], -part, SQ[0] if n == 0 else r,
                                                                                  ALU.mult, ALU.add))
                    own("trig_step", (l, i, "min"), nc.vector.tensor_scalar(r, r, shift, SIN_MAX, ALU.add, ALU.min))
                    own("trig_step", (l, i, "max"), nc.vector.tensor_scalar(r, r, -SIN_MAX, None, ALU.max))
                dve.wait_ge(*at("trig_act", (l, 3)))
                project(("mix_in", l), mixer_tiles(), FIRST["mix_in", l], SEQ, QK2, 0, ROPE2,
                        lambda t: DV[:, :, :] if t["kind"] == "dv" else VN2[:, :, t["col"]:t["col"] + P])
                stage_end()
                for m in range(2):
                    cb, cc, ch = (QK2[:, 13 + 2 * i + m, :] for i in range(3))
                    y = TMP[m]
                    own("cv_step", (l, m, "u"), nc.vector.tensor_tensor(cc, cc, ch, ALU.mult))
                    own("cv_step", (l, m, 2), nc.vector.tensor_scalar(y, cc, prm("conv_w_2", l * 6 + 4 + m), None, ALU.mult))
                    for back, tap in ((1, 1), (2, 0)):
                        own("cv_step", (l, m, tap), nc.vector.scalar_tensor_tensor(
                            y[:, back:SEQ], cc[:, 0:SEQ - back], prm("conv_w_2", l * 6 + 2 * tap + m), y[:, back:SEQ],
                            ALU.mult, ALU.add))
                    own("cv_step", (l, m, "y"), nc.vector.tensor_tensor(y, y, cb, ALU.mult))
                for m in range(2):
                    dve.wait_ge(*at("cv_hi", (l, m)))
                    lo("cv_step", (l, m, "lo"), HL[:, m, :], TMP[m], HH[:, m, :])
                dve.wait_ge(*at("bias2_in", (l, 5)))
                for h in range(6):
                    nc.vector.tensor_tensor(TBK[:, h, P:2 * P], TBK[:, h, P:2 * P], CAUSAL, ALU.add).then_inc(
                        *mark("bias_step", ("causal", l, h)))
                nc.vector.tensor_copy(DMASK[:, 0, 0:P], CAUSAL).then_inc(*mark("bias_step", ("first", l)))
                own("idx_step", (l, "weights"), nc.vector.tensor_scalar(IW[:, :, :], DV[:, :, 64:72], 8.0 ** -0.5, None,
                                                                       ALU.mult))
                for n, (t, h) in enumerate(INDEX_STEPS):
                    nk = (t + 1) * P
                    sc = SCORE[:, 0:nk]
                    dve.wait_ge(*at("idx_relu", (l, n)))
                    w = IW[:, t, h:h + 1]
                    if h == 0:
                        own("idx_step", (l, n), nc.vector.tensor_scalar(sc, SQ[n % 2][:, 0:nk], w, None, ALU.mult))
                        continue
                    own("idx_step", (l, n), nc.vector.scalar_tensor_tensor(sc, SQ[n % 2][:, 0:nk], w, sc, ALU.mult, ALU.add))
                    if h < 7:
                        continue
                    own("idx_step", (l, t, "causal"), nc.vector.tensor_tensor(SCORE[:, t * P:nk], SCORE[:, t * P:nk], CAUSAL,
                                                                             ALU.add))
                    for r in range(TOPK // 8):
                        own("idx_step", (l, t, r, "max"), nc.vector.max(TOP8[:, :], sc))
                        own("idx_step", (l, t, r, "out"), nc.vector.match_replace(sc, TOP8[:, :], sc, TAKEN))
                    own("idx_step", (l, t, "mask"), nc.vector.tensor_scalar(DMASK[:, t, 0:nk], sc, TAKEN / 2, NEG, ALU.is_gt,
                                                                           ALU.mult))
                stage_end()
                attend(number_attention(("att2", l), attention_units_2(l)))
                stage_end()
                out_proj(("mix_out", l), FIRST["mix_out", l], SEQ, XT, lambda k: None)
                stage_end()
                layer_norm(("ln1", l), mem=l)
                for n in range(KT, 2 * KT):
                    dve.wait_ge(*at("v_turned", (("mem_kv", l), n)))
                    nc.vector.tensor_copy(MV[:, :, (n - KT) * P:(n - KT + 1) * P],
                                          PS[:, 4 + n % 2, 0:MEM].rearrange("p (t c) -> p t c", c=P)).then_inc(
                                              *mark("v_copied", (("mem_kv", l), n)))
                stage_end()
                attend(number_attention(("att3", l), attention_units_3()))
                stage_end()
                out_proj(("mem_out", l), FIRST["mem_out", l], SEQ, XT, lambda k: None)
                stage_end()
                layer_norm(("ln2", l))
                ffn(("ff", l), FIRST["ff", l], SEQ, l, GROUPS_2, 1, XT, lambda k: None)
                stage_end()
                layer_norm(("ln3", l))


_INS = ['x', 'c', 'ctx', 'c_ctx', 'w_ada', 'b_ada', 'g_norm1', 'w_in', 'gq_a', 'gk_a', 'gq_b', 'gk_b', 'rpb_b', 'gq_c',
        'gk_c', 'lambda_q1', 'lambda_k1', 'lambda_q2', 'lambda_k2', 'g_subln', 'w_out', 'g_norm2', 'w_up', 'conv_w',
        'conv_b', 'w_down', 'mem_2', 'positions_2', 'w_in_2', 'conv_w_2', 'rel_bias_2', 'w_mix_out_2', 'ln1_g_2',
        'ln1_b_2', 'w_mq_2', 'w_mkv_2', 'w_mo_2', 'ln2_g_2', 'ln2_b_2', 'w_ff1_2', 'w_ff2_2', 'ln3_g_2', 'ln3_b_2']


def kernel(**inputs):
    import numpy as _np
    import concourse.bacc as _bacc
    from concourse import mybir as _mybir
    from concourse.bass_utils import run_bass_kernel_spmd as _run

    arrays = {name: _np.ascontiguousarray(inputs[name]) for name in _INS if name != "rel_bias_2"}
    arrays["rel_reversed"] = _np.ascontiguousarray(_np.asarray(inputs["rel_bias_2"])[:, :, ::-1])
    arrays.update(constant_arrays())

    def program(counts):
        nc = _bacc.Bacc("TRN2", target_bir_lowering=False, num_devices=1)
        aps = {name: nc.dram_tensor(f"in_{name}_dram", a.shape, _mybir.dt.from_np(a.dtype), kind="ExternalInput").ap()
               for name, a in arrays.items()}
        out = nc.dram_tensor("out_0_dram", (1, SEQ, D), F32, kind="ExternalOutput").ap()
        build(nc, aps, out, counts)
        return nc

    counts = {}
    program(counts)
    nc = program(counts)
    r = _run(nc, [{f"in_{name}_dram": a for name, a in arrays.items()}], core_ids=[0])
    return r.results[0]["out_0_dram"]
```

```python
import math
from contextlib import ExitStack

import numpy as np
import concourse.bass as bass
from concourse import mybir

F32 = mybir.dt.float32
F32R = mybir.dt.float32r
I32 = mybir.dt.int32
ALU = mybir.AluOpType
ACT = mybir.ActivationFunctionType
AX = mybir.AxisListType

P = 128
D = 1024
KT = D // P
SEQ = 512
CTX = 256
MEM = 256
DEPTH = 2
GRID_W = 64
HEAD = 64
WIN_W = 16
B_HEADS = 4
FFN = 2816
FT = FFN // P
EPS = 1e-6
LN_EPS = 1e-5
ALPHA = (2.0 * DEPTH) ** 0.25
D_FF = 4096
NEG = -1e30
TAKEN = -3e38
REL_CLIP, CHUNK = 128, 64
REL_SIZE = (CHUNK - 1) + REL_CLIP + 1
TOPK = 128
NRAW = 3
NSPLIT = 3
AHEAD = 2
NSUM = 4
LAG = 2


def axial_tables(dim):
    half = dim // 2
    inv = (10000.0 ** (-np.arange(0, half, 2, dtype=np.float32) / half)).astype(np.float32)
    t = np.arange(SEQ)
    row, col = (t // GRID_W).astype(np.float32), (t % GRID_W).astype(np.float32)
    ang = np.concatenate([row[:, None] * inv, col[:, None] * inv], axis=-1).astype(np.float32)
    full = np.tile(np.repeat(ang, 2, axis=1), (1, P // dim)).T
    return np.cos(full).astype(np.float32), np.sin(full).astype(np.float32)


def constant_arrays():
    i = np.arange(P)
    eye = (i[:, None] == i[None, :]).astype(np.float32)
    mean = np.full((P, P), 1.0 / D, np.float32)
    blk64 = (i[:, None] // 64 == i[None, :] // 64).astype(np.float32)
    blk32 = (i[:, None] // 32 == i[None, :] // 32).astype(np.float32)
    pair = np.zeros((P, P), np.float32)
    pair[i[::2] + 1, i[::2]] = -1.0
    pair[i[::2], i[::2] + 1] = 1.0
    half_d = np.zeros((P, P), np.float32)
    freq = np.zeros((P, 2), np.float32)
    half_i = np.zeros((P, P), np.float32)
    for mat, period, half, c in ((half_d, 64, 8, 0), (half_i, 32, 4, 1)):
        inv = np.power(np.float32(500000.0), -np.arange(half, dtype=np.float32) / half).astype(np.float32)
        for b in range(0, P, period):
            for j in range(half):
                mat[b + j + half, b + j] = -1.0
                mat[b + j, b + j + half] = 1.0
                freq[b + j, c] = freq[b + j + half, c] = inv[j]
    q = np.arange(P) % 64
    start = np.clip(q - WIN_W // 2, 0, GRID_W - WIN_W)
    kc = np.arange(GRID_W)
    inside = (kc[None, :] >= start[:, None]) & (kc[None, :] < start[:, None] + WIN_W)
    window = np.where(inside, 0.0, NEG).astype(np.float32)
    causal = np.where(i[None, :] // CHUNK <= i[:, None] // CHUNK, 0.0, NEG).astype(np.float32)
    pack = np.concatenate([eye, mean, blk64, blk32, pair, half_d, half_i, causal, window, freq], axis=1)
    ca, sa = axial_tables(64)
    cc, sc = axial_tables(32)
    return {"const_pack": pack, "const_rope": np.stack([ca, sa, cc, sc], axis=1)}


def param_columns():
    cols, n = {}, 0
    for name, rows in (("b_ada", 2 * 48), ("g_norm1", 16), ("g_norm2", 16), ("conv_w", 2 * 3 * 2 * FT),
                       ("conv_b", 2 * 2 * FT), ("conv_w_2", 2 * 3 * 2), ("ln1_g_2", 16), ("ln1_b_2", 16),
                       ("ln2_g_2", 16), ("ln2_b_2", 16), ("ln3_g_2", 16), ("ln3_b_2", 16), ("c", 8),
                       ("c_ctx", 8), ("gains", 12)):
        cols[name] = (n, rows)
        n += rows
    return cols, n


PCOL, NPARAM = param_columns()
NGRP = -(-NPARAM // P)
GAINS = ("gq_a", "gk_a", "gq_b", "gk_b", "gq_c", "gk_c")


def weight_chunks():
    chunks, first = [], {}

    def add(key, name, layer, k0, nk, pieces):
        first.setdefault(key, len(chunks))
        chunks.append((name, layer, k0, nk, pieces))

    def cols(c):
        return [(0, P, c)]

    for l in range(DEPTH):
        for n in range(48):
            add(("ada", l), "w_ada", l, 0, KT, cols(n * P))
    for l in range(DEPTH):
        for s in ("c", "x"):
            for tile in qkv_tiles(s, l):
                add(("qkv", s, l), "w_in", l, 0, KT, tile["pieces"])
        for s in streams(l):
            for n in range(KT):
                add(("out", s, l), "w_out", l, 0, KT, cols(n * P))
        for s in streams(l):
            for step in ffn_steps(GROUPS_1, 2):
                if step[0] == "up":
                    _, g, j, part = step
                    add(("ffn", s, l), "w_up", l, 0, KT, cols(part * FFN + (GROUPS_1[g][0] + j) * P))
                else:
                    _, g, n = step
                    add(("ffn", s, l), "w_down", l, GROUPS_1[g][0], GROUPS_1[g][1], cols(n * P))
    for l in range(DEPTH):
        for tile in mixer_tiles():
            add(("mix_in", l), "w_in_2", l, 0, KT, tile["pieces"])
        for n in range(KT):
            add(("mix_out", l), "w_mix_out_2", l, 0, KT, cols(n * P))
        for n in range(2 * KT):
            add(("mem_kv", l), "w_mkv_2", l, 0, KT, cols(n * P))
        for n in range(KT):
            add(("mem_q", l), "w_mq_2", l, 0, KT, cols(n * P))
        for n in range(KT):
            add(("mem_out", l), "w_mo_2", l, 0, KT, cols(n * P))
        for step in ffn_steps(GROUPS_2, 1):
            if step[0] == "up":
                _, g, j, _ = step
                add(("ff", l), "w_ff1_2", l, 0, KT, cols((GROUPS_2[g][0] + j) * P))
            else:
                _, g, n = step
                add(("ff", l), "w_ff2_2", l, GROUPS_2[g][0], GROUPS_2[g][1], cols(n * P))
    return chunks, first


def streams(layer):
    return ("x", "c")[:DEPTH - layer]


TOKENS = {"x": SEQ, "c": CTX}
GROUPS_1 = [(0, 8), (8, 8), (16, 6)]
GROUPS_2 = [(0, 8), (8, 8), (16, 8), (24, 8)]


def ffn_steps(groups, parts):
    steps = []
    for g in range(len(groups) + 1):
        if g < len(groups):
            steps += [("up", g, j, part) for j in range(groups[g][1]) for part in range(parts)]
        if g:
            steps += [("down", g - 1, n) for n in range(KT)]
    return steps


def qkv_tiles(stream, layer):
    only_kv = stream == "c" and layer == DEPTH - 1
    tiles = []

    def qk(slot, gain, blk, rope, pieces):
        if gain % 2 or not only_kv:
            tiles.append(dict(kind="qk", slot=slot, gain=gain, blk=blk, rope=rope, pieces=pieces))

    for m in range(4):
        qk(m, 0, 0, 0, [(0, 64, 64 * m), (64, 64, 256 + 64 * m)])
    qk(4, 1, 0, 0, [(0, P, 512)])
    for m in range(2):
        qk(5 + m, 2, 0, None, [(0, P, 768 + P * m)])
        qk(7 + m, 3, 0, None, [(0, P, 1024 + P * m)])
    for m in range(2):
        qk(9 + m, 4, 1, 2, [(0, P, 1536 + P * m)])
        qk(11 + m, 5, 1, 2, [(0, P, 1792 + P * m)])
    for n, c in enumerate((640, 1280, 1408, 2048, 2176)):
        tiles.append(dict(kind="v", col=n * P, pieces=[(0, P, c)]))
    if stream == "c":
        for t in tiles:
            t["rope"] = None
    return tiles


def is_value(tile):
    return tile["kind"] in ("v", "dv")


def aux_before(tiles, j):
    before = [m for m in range(j) if m % 2 == j % 2 and ("blk" in tiles[m] or is_value(tiles[m]))]
    return before[-1] if before else None


def mixer_tiles():
    t = [dict(kind="qk", slot=4 + m, rope=2, scale=1.0, pieces=[(0, P, 1280 + P * m)]) for m in range(2)]
    t.append(dict(kind="qk", slot=6, rope=2, scale=1.0, pieces=[(32 * j, 32, 1536) for j in range(4)]))
    t.append(dict(kind="dv", pieces=[(0, 64, 1216), (64, 64, 1568)]))
    t += [dict(kind="qk", slot=m, rope=0, scale=0.125, pieces=[(0, P, 768 + P * m)]) for m in range(3)]
    t.append(dict(kind="qk", slot=3, rope=0, scale=1.0, pieces=[(0, 64, 1152), (64, 64, 1152)]))
    t += [dict(kind="plain", slot=13 + m, scale=1.0, pieces=[(0, P, P * m)]) for m in range(6)]
    t += [dict(kind="plain", slot=7 + m, scale=0.125, pieces=[(0, P, 1576 + P * m)]) for m in range(3)]
    t += [dict(kind="plain", slot=10 + m, scale=1.0, pieces=[(0, P, 1960 + P * m)]) for m in range(3)]
    t += [dict(kind="v", col=m * P, pieces=[(0, P, 2344 + P * m)]) for m in range(3)]
    return t


CHUNKS, FIRST = weight_chunks()


def is_split(c):
    return CHUNKS[c][0] != "w_ada"


INDEX_STEPS = [(t, h) for t in (3, 2, 1) for h in range(8)]
INDEX_FIRST, CONV_STEP = 5, 17


def index_logits(step):
    return [n for n in (2 * (step - INDEX_FIRST), 2 * (step - INDEX_FIRST) + 1) if 0 <= n < len(INDEX_STEPS)]


def index_rounds(step):
    n = step - INDEX_FIRST - 4
    return (3 - n // 4, 4 * (n % 4), 4) if 0 <= n < 12 else None


ROUND = 12582912.0
TWO_PI_PARTS = (6.28125, float(np.float32(0.00193500518798828125)), 2 * math.pi - 6.28125 - 0.00193500518798828125)
SIN_MAX = 3.1415925


def build(nc, A, out, counts):
    ctx = ExitStack()
    totals = {}
    sems = {}

    def sem(name):
        sems[name] = ctx.enter_context(nc.semaphore(name))
        return name

    def mark(name, key, by=1):
        totals[name] = totals.get(name, 0) + by
        assert (name, key) not in marked, (name, key)
        marked.add((name, key))
        counts[name, key] = totals[name]
        return sems[name], by

    def at(name, key):
        if strict:
            return sems[name], counts[name, key]
        return sems[name], counts.get((name, key), 1)

    marked = set()
    strict = bool(counts)

    with ctx:
        def sb(name, shape, dt=F32, where=ctx):
            return where.enter_context(nc.sbuf_tensor(name, shape, dt))

        XT = sb("x_t", [P, KT, SEQ])
        CT = sb("ctx_t", [P, KT, CTX])
        HH = sb("h_hi", [P, KT, SEQ], F32R)
        HL = sb("h_lo", [P, KT, SEQ], F32R)
        RAW = sb("w_raw", [P, NRAW, KT, P])
        WH = sb("w_hi", [P, NSPLIT, KT, P], F32R)
        WL = sb("w_lo", [P, NSPLIT, KT, P], F32R)
        ACC = sb("acc", [P, SEQ])
        RSTD = sb("rstd", [P, SEQ])
        WORK = sb("work", [P, 4 * 768])
        PACK = sb("const_sb", [P, 8 * P + 64 + 2])
        PRM = sb("params", [P, NGRP, P])
        MOD = sb("mod", [P, DEPTH, 48, 2])
        GMOD = sb("gain_mod", [P, DEPTH, 2, 2, KT])
        SILU = sb("silu_c", [P, KT, 2])
        HG = sb("head_gain", [P, 2, 6])
        LAM = sb("lam", [P, 2, 4])
        GSUB = sb("g_sub", [P, 2, HEAD])
        RELC = sb("rel_const", [P, 12])
        EPSC = sb("eps_cols", [P, 4])
        NMAX = sb("neg_max", [P, 4])
        SUMS = sb("prob_sums", [P, NSUM, 16])
        RSUM = sb("recip_sums", [P, 2, 16])
        COEF = sb("diff_coef", [P, 4])
        SSQ = sb("sub_sumsq", [P, 2, 4])
        TOP8 = sb("top8", [P, 8])
        IW = sb("idx_weights", [P, 4, 8])
        PS = ctx.enter_context(nc.psum_tensor("psum", [P, 8, 512], F32))

        IDENT, MEAN, BLK64, BLK32, PAIR, HALF_D, HALF_I, CAUSAL = (PACK[:, i * P:(i + 1) * P] for i in range(8))
        WINDOW = PACK[:, 8 * P:8 * P + 64]
        FREQ = PACK[:, 8 * P + 64:8 * P + 66]
        BLK = (BLK64, BLK32)
        SQ = [WORK[:, 512 * i:512 * i + 512] for i in range(2)]
        TMP = [WORK[:, 1024 + 512 * i:1536 + 512 * i] for i in range(2)]
        PROBS = {width: [WORK[:, width * i:width * (i + 1)] for i in range(4 * 768 // width)] for width in (512, 768)}

        def prm(name, i):
            c = PCOL[name][0] + i
            return PRM[:, c // P, c % P:c % P + 1]

        def prm_range(name, i, n):
            c = PCOL[name][0] + i
            return PRM[:, :, :].rearrange("p g c -> p (g c)")[:, c:c + n]

        ph = ExitStack()
        XN = sb("x_nat", [P, 6, D], where=ph)
        PROWS = sb("param_rows", [P, NGRP, P], where=ph)
        RPBR = sb("rpb_rows", [120, P], where=ph)
        RELR = sb("rel_rows", [12, 384], where=ph)
        MROW = sb("mod_rows_sb", [2, 2 * 6 * D], where=ph)
        LAMV = sb("lam_vec", [P, 2, 4, 32], where=ph)
        ph.close()
        ph = ExitStack()
        QK = sb("qk_t", [P, 13, SEQ + CTX], where=ph)
        VN = sb("v_nat", [P, 6, 640], where=ph)
        TB = sb("win_bias", [P, B_HEADS, 14, GRID_W], where=ph)
        ROPE = sb("rope_1", [P, 4, SEQ], where=ph)
        PT = sb("probs_t", [P, 2, 6 * P], where=ph)
        ON = sb("o_nat", [P, 2, D], where=ph)
        ph.close()
        ph = ExitStack()
        GH = sb("hid_hi", [P, 2, 8, SEQ], F32R, where=ph)
        GL = sb("hid_lo", [P, 2, 8, SEQ], F32R, where=ph)
        MU = sb("mid_u", [P, 3, SEQ], where=ph)
        MG = sb("mid_g", [P, 3, SEQ], where=ph)
        ph.close()
        ph = ExitStack()
        QK2 = sb("qk_t_2", [P, 19, SEQ], where=ph)
        VN2 = sb("v_nat_2", [P, 4, 384], where=ph)
        DV = sb("dv_nat", [P, 4, P], where=ph)
        TBK = sb("rel_bias_t", [P, 6, 256], where=ph)
        DMASK = sb("sel_mask", [P, 4, SEQ], where=ph)
        PT2 = sb("probs_t_2", [P, 2, 4 * P], where=ph)
        ON2 = sb("o_nat_2", [P, 2, 768], where=ph)
        POSI = sb("pos_int", [P, SEQ], I32, where=ph)
        FFN_BYTES = 4 * SEQ * (4 * 8 + 2 * 3)
        MIX_BYTES = 4 * ((19 + 4 + 1) * SEQ + 4 * 384 + 4 * P + 6 * 256 + 2 * 4 * P + 2 * 768)
        sb("gap", [P, (FFN_BYTES - MIX_BYTES) // 4], where=ph)
        ROPE2 = sb("rope_2", [P, 4, SEQ], where=ph)
        ph.close()
        ph = ExitStack()
        MQ = sb("mem_q_t", [P, KT, SEQ], where=ph)
        MK = sb("mem_k_t", [P, KT, MEM], where=ph)
        MV = sb("mem_v", [P, 2, D], where=ph)
        MH = sb("mem_hi", [P, KT, MEM], F32R, where=ph)
        ML = sb("mem_lo", [P, KT, MEM], F32R, where=ph)
        PT3 = sb("probs_t_3", [P, 2, 2 * P], where=ph)
        ON3 = sb("o_nat_3", [P, 2, D], where=ph)
        ph.close()
        ph = ExitStack()
        OUTS = sb("out_nat", [P, 4, D], where=ph)
        ph.close()

        RPB_PAD = nc.dram_tensor("rpb_pad", (120, 64, P), F32).ap()
        REL_PAD = nc.dram_tensor("rel_pad", (12, P, 384), F32).ap()

        for i in range(NRAW):
            sem(f"w_loaded{i}")
        for name in ("w_hi", "w_lo", "w_used", "stage_end", "consts_in", "rows_in", "acts_in", "mem_in", "bias_in",
                     "tab_in", "bias2_in", "pad_written", "zeroed", "x_ready", "mod_rows", "v_turned", "mem_hi_made", "mem_lo_made", "turned", "turned_taken", "param_step", "param_act",
                     "ada_done", "sq_ready", "sum_step", "stat_done", "std_ready", "norm_step", "norm_mid", "h_hi", "h_lo",
                     "lin_done", "raw_copied", "raw_squared", "v_copied", "blk_done", "blk_std", "qk_step",
                     "rot_done", "rope_step", "scores_done", "bias_step", "neg_max", "exp_done", "mix_step", "probs_turned_a",
                     "probs_turned_b", "pt_copied_a", "pt_copied_b", "pv_done", "o_step", "sub_std", "o_turned_a",
                     "o_turned_b", "o_hi", "o_lo", "resid", "mid_ready", "conv_step", "silu_ready", "prod_ready", "hid_hi",
                     "hid_lo", "down_done", "trig_step", "trig_act", "idx_done", "idx_relu", "idx_step",
                     "cv_step", "cv_hi", "out_turned", "out_copied", "out_stored"):
            sem(name)

        block = ctx.enter_context(nc.Block())

        @block.sync
        def _(sp):
            for c, (name, layer, k0, nk, pieces) in enumerate(CHUNKS):
                if c >= NRAW:
                    sp.wait_ge(*at("w_lo" if is_split(c - NRAW) else "w_used", c - NRAW))
                for n, (dst, width, src) in enumerate(pieces):
                    w = A[name][layer, k0 * P:(k0 + nk) * P, src:src + width].rearrange("(k p) n -> p k n", p=P)
                    key = c if n == len(pieces) - 1 else (c, n)
                    sp.dma_start(RAW[:, c % NRAW, 0:nk, dst:dst + width], w).then_inc(
                        *mark(f"w_loaded{c % NRAW}", key, 16))

        @block.gpsimd
        def _(pool):
            for c, (_, _, _, nk, _) in enumerate(CHUNKS):
                if not is_split(c):
                    continue
                pool.wait_ge(*at("w_hi", c))
                nc.gpsimd.tensor_tensor(WL[:, c % NSPLIT, 0:nk, :], RAW[:, c % NRAW, 0:nk, :],
                                        WH[:, c % NSPLIT, 0:nk, :].bitcast(F32), ALU.subtract).then_inc(
                                            *mark("w_lo", c))

        def lin_bank(i):
            return i % 4

        def wide(values, col, head):
            fits = col + P <= values.shape[1] and (head + 2) * HEAD <= 512
            return values[:, col:col + (P if fits else HEAD)]

        def attention_units_1(stream, layer):
            units, groups = [], []
            tiles = range(4) if stream == "x" else range(2)
            nk = SEQ + CTX if stream == "x" else CTX
            k0 = 0 if stream == "x" else SEQ
            vt = range(6) if stream == "x" else range(4, 6)
            q0 = 0 if stream == "x" else SEQ
            for t in tiles:
                qc = slice(q0 + t * P, q0 + (t + 1) * P)

                def one(slot_q, slot_k, part, rows):
                    return [(QK[part:part + rows, slot_q, qc], QK[part:part + rows, slot_k, k0:k0 + nk])]

                for h in range(8):
                    part, slot = 64 * (h // 4), h % 4
                    units.append(dict(maps=[one(slot, 4, part, 64)], nk=nk, adds=[],
                                      v=[wide(VN[:, j, :], 64 * (h // 4), h) for j in vt],
                                      t=t, group=len(groups), head=h, dv=64, last=h == 7))
                groups.append(dict(heads=8, dv=64, col=0, diff=False))
                for h in range(4):
                    part = 64 * (h % 2)
                    adds = []
                    if stream == "x":
                        bias = TB[:, h, 6 - 2 * t:14 - 2 * t, :].rearrange("p a b -> p (a b)")
                        adds = [(0, SEQ, bias)]
                    units.append(dict(maps=[one(5 + h // 2, 7 + h // 2, part, 64)], nk=nk, adds=adds,
                                      v=[wide(VN[:, j, :], P + 64 * h, h) for j in vt],
                                      t=t, group=len(groups), head=h, dv=64, last=h == 3))
                groups.append(dict(heads=4, dv=64, col=512, diff=False))
                for h in range(4):
                    part = 64 * (h % 2)
                    units.append(dict(maps=[one(9 + h // 2, 11 + h // 2, part + 32 * m, 32) for m in range(2)],
                                      nk=nk, adds=[], v=[wide(VN[:, j, :], 384 + 64 * h, h) for j in vt],
                                      t=t, group=len(groups), head=h, dv=64, last=h == 3))
                groups.append(dict(heads=4, dv=64, col=768, diff=True, layer=layer))
                units[-1]["tile_last"] = True
            return dict(units=units, groups=groups, PT=PT, ON=ON, tiles=8, first=0)

        def attention_units_2(layer):
            units, groups = [], []
            for t in range(4):
                nk = P * (t + 1)
                qc = slice(t * P, (t + 1) * P)
                for h in range(6):
                    part = 64 * (h % 2)
                    units.append(dict(maps=[[(QK2[part:part + 64, 7 + h // 2, qc], QK2[part:part + 64, 10 + h // 2, 0:nk])]],
                                      nk=nk,
                                      adds=([(0, P, TBK[:, h, P:2 * P])] if t == 0 else
                                            ([(0, nk - 2 * P, RELC[:, layer * 6 + h:layer * 6 + h + 1])] if t > 1 else [])
                                            + [(nk - 2 * P, nk, TBK[:, h, :])]),
                                      v=[wide(VN2[:, j, :], 64 * h, h) for j in range(t + 1)],
                                      t=t, group=len(groups), head=h, dv=64, last=h == 5))
                groups.append(dict(heads=6, dv=64, col=384, diff=False))
                for h in range(6):
                    part = 64 * (h % 2)
                    units.append(dict(maps=[[(QK2[part:part + 64, h // 2, qc], QK2[part:part + 64, 3, 0:nk])]],
                                      nk=nk, adds=[(0, nk, DMASK[:, t, 0:nk])],
                                      v=[wide(DV[:, j, :], 0, h) for j in range(t + 1)],
                                      t=t, group=len(groups), head=h, dv=64, last=h == 5))
                groups.append(dict(heads=6, dv=64, col=0, diff=False))
                units[-1]["tile_last"] = True
            return dict(units=units, groups=groups, PT=PT2, ON=ON2, tiles=6, first=2)

        def attention_units_3():
            units, groups = [], []
            for t in range(4):
                qc = slice(t * P, (t + 1) * P)
                for h in range(4):
                    units.append(dict(maps=[[(MQ[:, 2 * h + i, qc], MK[:, 2 * h + i, :]) for i in range(2)]],
                                      nk=MEM, adds=[], v=[MV[:, j, 256 * h:256 * h + 256] for j in range(2)],
                                      t=t, group=len(groups), head=h % 2, dv=256, last=h % 2 == 1))
                    if h % 2:
                        groups.append(dict(heads=2, dv=256, col=256 * (h - 1), diff=False))
                units[-1]["tile_last"] = True
            return dict(units=units, groups=groups, PT=PT3, ON=ON3, tiles=8, first=0)

        def number_attention(S, att):
            n, uses = 0, {}
            units = att["units"]
            att["wide"] = units[-1]["nk"] > 512
            att["nscore"] = 2 if att["wide"] else 4
            att["prob"] = PROBS[768 if att["wide"] else 512]
            att["lag"] = lag = LAG + (1 if not att["wide"] and all(len(u["maps"]) == 1 for u in units) else 0)
            for u, unit in enumerate(units):
                unit["sub"] = list(range(n, n + len(unit["maps"])))
                n += len(unit["maps"])
            k = 0
            for i in range(len(units) + lag + 4):
                if 0 <= i - lag < len(units):
                    uses["unit", i - lag] = k
                    k += 1
                j = i - lag - 3
                if 0 <= j < len(units) and units[j].get("tile_last"):
                    uses["tile", units[j]["t"]] = k
                    k += 1
            att["S"], att["uses"], att["order"] = S, uses, {v: k for k, v in uses.items()}
            return att

        def scores(att, s):
            step, b = (2, 2 * (s % 2)) if att["wide"] else (1, s % 4)
            return PS[:, b:b + step, :].rearrange("p b c -> p (b c)")

        def turn_bank(att, j):
            return 4 if att["wide"] else 4 + j % 2

        @block.tensor
        def _(pe):
            stage = [0]

            def stage_end():
                stage[0] += 1
                pe.drain().then_inc(*mark("stage_end", ("pe", stage[0])))
                pe.wait_ge(sems["stage_end"], 3 * stage[0])

            def product(out_ap, lhs, rhs, nk):
                for k in range(nk):
                    for n, (a, b) in enumerate(((0, 0), (0, 1), (1, 0))):
                        m = pe.matmul(out_ap, lhs(a, k), rhs(b, k), start=(k == 0 and n == 0),
                                      stop=(k == nk - 1 and n == 2))
                return m

            def weights(c):
                w = (WH[:, c % NSPLIT], WL[:, c % NSPLIT])
                pe.wait_ge(*at("w_lo", c))
                return w

            def tile_t(c, out_ap, acts, T, nk=KT):
                w = weights(c)
                product(out_ap, lambda a, k: w[a][:, k, :], lambda b, k: acts[b][:, k, 0:T], nk).then_inc(
                    *mark("w_used", c))

            H = (HH, HL)

            def turn_in(S, n):
                for i in range(n):
                    for half in range(2):
                        b = (2 * i + half) % 8
                        if 2 * i + half >= 8:
                            pe.wait_ge(*at("turned_taken", (S, 2 * i + half - 8)))
                        for k in range(4):
                            m = pe.transpose(PS[:, b, k * P:(k + 1) * P], XN[:, i, (4 * half + k) * P:(4 * half + k + 1) * P],
                                             IDENT)
                        m.then_inc(*mark("turned", (S, 2 * i + half)))

            def stat(S, T, bank=0):
                pe.wait_ge(*at("sum_step", (S, "total")))
                pe.matmul(PS[:, bank, 0:T], MEAN, ACC[:, 0:T], start=True, stop=True).then_inc(
                    *mark("stat_done", S))

            def aux_bank_free(S, tiles, j):
                p = aux_before(tiles, j)
                if p is not None:
                    pe.wait_ge(*at("v_copied" if is_value(tiles[p]) else "blk_std", (S, p)))

            def turn_values(S, j, T):
                for t in range(T // P):
                    m = pe.transpose(PS[:, 4 + j % 2, t * P:(t + 1) * P], SQ[j % 2][:, t * P:(t + 1) * P], IDENT)
                m.then_inc(*mark("v_turned", (S, j)))

            def project(S, tiles, c0, T, rots, beside=lambda i: None):
                n = len(tiles)
                for i in range(n + 2):
                    beside(i - 1)
                    if i < n:
                        if i >= 4:
                            pe.wait_ge(*at("raw_copied", (S, i - 4)))
                        tile_t(c0 + i, PS[:, lin_bank(i), 0:T], H, T)
                    j = i - 1
                    if 0 <= j < n and tiles[j]["kind"] == "qk" and "blk" in tiles[j]:
                        pe.wait_ge(*at("raw_squared", (S, j)))
                        aux_bank_free(S, tiles, j)
                        pe.matmul(PS[:, 4 + j % 2, 0:T], BLK[tiles[j]["blk"]], SQ[j % 2][:, 0:T], start=True,
                                  stop=True).then_inc(*mark("blk_done", (S, j)))
                    if 0 <= j < n and is_value(tiles[j]):
                        pe.wait_ge(*at("raw_copied", (S, j)))
                        aux_bank_free(S, tiles, j)
                        if S[0] == "mix_in" and j > INDEX_FIRST:
                            pe.wait_ge(*at("idx_relu", (S[1], len(INDEX_STEPS) - 1)))
                        turn_values(S, j, T)
                    j = i - 2
                    if 0 <= j < n and tiles[j]["kind"] == "qk" and tiles[j]["rope"] is not None:
                        if "blk" in tiles[j]:
                            pe.wait_ge(*at("qk_step", (S, j, "norm")))
                        else:
                            pe.wait_ge(*at("raw_copied", (S, j)))
                        prev = [m for m in range(j) if tiles[m]["kind"] == "qk" and tiles[m]["rope"] is not None
                                and m % 2 == j % 2]
                        if prev:
                            pe.wait_ge(*at("rope_step", (S, prev[-1], "sin")))
                        dst, off = (QK, SEQ if S[1] == "c" else 0) if len(S) > 2 else (QK2, 0)
                        pe.matmul(PS[:, 6 + j % 2, 0:T], rots[tiles[j]["rope"]], dst[:, tiles[j]["slot"], off:off + T],
                                  start=True, stop=True).then_inc(*mark("rot_done", (S, j)))

            def out_proj(S, c0, T):
                for n in range(KT):
                    if n >= 4:
                        pe.wait_ge(*at("resid", (S, n - 4)))
                    tile_t(c0 + n, PS[:, lin_bank(n), 0:T], H, T)

            def attend(att):
                S, units, groups, PTt, ONt = att["S"], att["units"], att["groups"], att["PT"], att["ON"]
                uses, order, lag, nscore = att["uses"], att["order"], att["lag"], att["nscore"]

                def bank_free(use, bank):
                    for prev in range(use - 1, -1, -1):
                        kind, idx = order[prev]
                        if kind == "tile":
                            pe.wait_ge(*at("o_lo", (S, idx, "ab"[bank - 4])))
                            return
                        if att["wide"] or turn_bank(att, idx) == bank:
                            pe.wait_ge(*at("pt_copied_b" if att["wide"] and bank == 5 else "pt_copied_a", (S, idx)))
                            return

                for i in range(len(units) + lag + 4):
                    if i < len(units):
                        u = units[i]
                        for s, pieces in zip(u["sub"], u["maps"]):
                            if s >= nscore:
                                pe.wait_ge(*at("exp_done", (S, s - nscore)))
                            for lo in range(0, u["nk"], 512):
                                hi = min(lo + 512, u["nk"])
                                for n, (q, k) in enumerate(pieces):
                                    m = pe.matmul(scores(att, s)[:, lo:hi], q, k[:, lo:hi],
                                                  start=n == 0, stop=n == len(pieces) - 1)
                            m.then_inc(*mark("scores_done", (S, s)))
                    j = i - lag
                    if 0 <= j < len(units):
                        u = units[j]
                        if len(u["sub"]) == 2:
                            pe.wait_ge(*at("mix_step", (S, j, "mixed")))
                        else:
                            pe.wait_ge(*at("exp_done", (S, u["sub"][0])))
                        use = uses["unit", j]
                        bank_free(use, turn_bank(att, j))
                        src = att["prob"][u["sub"][-1] % len(att["prob"])]
                        for kt in range(u["nk"] // P):
                            if kt == 4:
                                bank_free(use, 5)
                            m = pe.transpose(PS[:, turn_bank(att, j) + kt // 4, (kt % 4) * P:(kt % 4 + 1) * P],
                                             src[:, kt * P:(kt + 1) * P], IDENT)
                            if kt == min(4, u["nk"] // P) - 1:
                                m.then_inc(*mark("probs_turned_a", (S, j)))
                        if u["nk"] > 512:
                            m.then_inc(*mark("probs_turned_b", (S, j)))
                    j = i - lag - 1
                    if 0 <= j < len(units):
                        u = units[j]
                        pe.wait_ge(*at("pt_copied_a", (S, j)))
                        if u["nk"] > 512:
                            pe.wait_ge(*at("pt_copied_b", (S, j)))
                        g = u["group"]
                        if u["head"] == 0 and g >= 2:
                            pe.wait_ge(*at("o_step", (S, g - 2, "scaled")))
                        col = u["head"] * u["dv"]
                        for kt, v in enumerate(u["v"]):
                            m = pe.matmul(PS[:, 6 + g % 2, col:col + v.shape[1]],
                                          PTt[:, j % 2, kt * P:(kt + 1) * P], v, start=kt == 0,
                                          stop=kt == len(u["v"]) - 1)
                        m.then_inc(*mark("pv_done", (S, j)))
                    j = i - lag - 3
                    if 0 <= j < len(units) and units[j].get("tile_last"):
                        t = units[j]["t"]
                        g = units[j]["group"]
                        pe.wait_ge(*at("o_step", (S, g, "ready" if groups[g]["diff"] else "scaled")))
                        bank_free(uses["tile", t], 4)
                        for k in range(att["tiles"]):
                            if k == 4:
                                bank_free(uses["tile", t], 5)
                            m = pe.transpose(PS[:, 4 + k // 4, (k % 4) * P:(k % 4 + 1) * P],
                                             ONt[:, t % 2, k * P:(k + 1) * P], IDENT)
                            if k == 3:
                                m.then_inc(*mark("o_turned_a", (S, t)))
                        m.then_inc(*mark("o_turned_b", (S, t)))

            def ffn(S, c0, T, groups, parts):
                up = 0
                down = 0
                for n, step in enumerate(ffn_steps(groups, parts)):
                    if step[0] == "up":
                        if up >= 4:
                            if parts == 2:
                                pe.wait_ge(*at("conv_step", (S, up - 4, "after")))
                            else:
                                pe.wait_ge(*at("mid_ready", (S, up - 4)))
                        tile_t(c0 + n, PS[:, lin_bank(up), 0:T], H, T)
                        up += 1
                    else:
                        _, g, m = step
                        if down >= 4:
                            pe.wait_ge(*at("resid", (S, down - 4)))
                        if m == 0:
                            pe.wait_ge(*at("hid_lo", (S, groups[g][0] + groups[g][1] - 1)))
                        tile_t(c0 + n, PS[:, 4 + down % 4, 0:T], (GH[:, g % 2], GL[:, g % 2]), T, groups[g][1])
                        down += 1

            def layer_norm(S, mem_tiles=None):
                stat((S, "mean"), SEQ, 6)
                if mem_tiles is not None:
                    mem_tiles(range(3))
                stat((S, "var"), SEQ, 7)
                if mem_tiles is not None:
                    mem_tiles(range(3, 4))
                stage_end()

            pe.wait_ge(*at("consts_in", "last"))
            pe.wait_ge(*at("rows_in", "last"))
            for g in range(NGRP):
                m = pe.transpose(PS[:, 6 + g // 4, (g % 4) * P:(g % 4 + 1) * P], PROWS[:, g, :], IDENT)
            m.then_inc(*mark("turned", "params"))
            pe.wait_ge(*at("turned_taken", "params"))
            pe.wait_ge(*at("param_act", "silu"))
            for n in range(2 * 48):
                c = FIRST["ada", 0] + n
                if n % 4 == 0 and n >= 32:
                    pe.wait_ge(*at("mod_rows", n // 4 - 8))
                pe.wait_ge(*at(f"w_loaded{c % NRAW}", c))
                for k in range(KT):
                    m = pe.matmul(PS[0:2, n // 4 % 8, n % 4 * P:(n % 4 + 1) * P], SILU[:, k, :], RAW[:, c % NRAW, k, :],
                                  start=k == 0, stop=k == KT - 1)
                m.then_inc(*mark("w_used", c))
            pe.wait_ge(*at("mod_rows", 23))
            for n in range(2 * 48):
                m = pe.transpose(PS[:, n // 48, 2 * (n % 48):2 * (n % 48) + 2], MROW[:, n * P:(n + 1) * P],
                                 IDENT[0:2, 0:2])
            m.then_inc(*mark("turned", "mod"))
            pe.wait_ge(*at("acts_in", "last"))
            pe.wait_ge(*at("param_step", ("mod", 1)))
            turn_in("in", 6)
            stage_end()
            for l in range(DEPTH):
                for s in ("c", "x"):
                    stat(("n1", s, l), TOKENS[s])
                    stage_end()
                    project(("qkv", s, l), qkv_tiles(s, l), FIRST["qkv", s, l], TOKENS[s], {0: PAIR, 2: PAIR})
                    stage_end()
                for s in streams(l):
                    attend(number_attention(("att", s, l), attention_units_1(s, l)))
                    stage_end()
                    out_proj(("out", s, l), FIRST["out", s, l], TOKENS[s])
                    stage_end()
                for s in streams(l):
                    stat(("n2", s, l), TOKENS[s])
                    stage_end()
                    ffn(("ffn", s, l), FIRST["ffn", s, l], TOKENS[s], GROUPS_1, 2)
                    stage_end()
            pe.wait_ge(*at("mem_in", "last"))
            turn_in("mem", 2)
            stage_end()
            for l in range(DEPTH):
                def logits(step):
                    for n in index_logits(step):
                        t, h = INDEX_STEPS[n]
                        if n == 0:
                            pe.wait_ge(*at("rope_step", (("mix_in", l), 2, "sum")))
                            pe.wait_ge(*at("v_copied", (("mix_in", l), 3)))
                        if n >= 2:
                            pe.wait_ge(*at("idx_relu", (l, n - 2)))
                        pp = 32 * (h % 4)
                        pe.matmul(PS[:, 4 + n % 2, 0:(t + 1) * P], QK2[pp:pp + 32, 4 + h // 4, t * P:(t + 1) * P],
                                  QK2[pp:pp + 32, 6, 0:(t + 1) * P], start=True, stop=True).then_inc(
                                      *mark("idx_done", (l, n)))

                project(("mix_in", l), mixer_tiles(), FIRST["mix_in", l], SEQ, {0: HALF_D, 2: HALF_I}, logits)
                stage_end()
                attend(number_attention(("att2", l), attention_units_2(l)))
                stage_end()
                out_proj(("mix_out", l), FIRST["mix_out", l], SEQ)
                stage_end()
                kv = ("mem_kv", l)

                def mem_tiles(ns):
                    for n in ns:
                        tile_t(FIRST[kv] + n, PS[:, lin_bank(n), 0:MEM], (MH, ML), MEM)

                layer_norm(("ln1", l), mem_tiles)
                for n in range(4, 2 * KT + 1):
                    pe.wait_ge(*at("raw_copied", (kv, n - 4)))
                    if n < 2 * KT:
                        mem_tiles([n])
                    if n > KT:
                        pe.wait_ge(*at("raw_copied", (kv, n - 1)))
                        if n > KT + 2:
                            pe.wait_ge(*at("v_copied", (kv, n - 3)))
                        turn_values(kv, n - 1, MEM)
                for n in range(KT):
                    pe.wait_ge(*(at("raw_copied", (kv, 2 * KT - 4 + n)) if n < 4 else
                                 at("raw_copied", (("mem_q", l), n - 4))))
                    tile_t(FIRST["mem_q", l] + n, PS[:, lin_bank(n), 0:SEQ], H, SEQ)
                stage_end()
                attend(number_attention(("att3", l), attention_units_3()))
                stage_end()
                out_proj(("mem_out", l), FIRST["mem_out", l], SEQ)
                stage_end()
                layer_norm(("ln2", l))
                ffn(("ff", l), FIRST["ff", l], SEQ, GROUPS_2, 1)
                stage_end()
                layer_norm(("ln3", l))
            for i in range(8):
                for k in range(4):
                    m = pe.transpose(PS[:, i, k * P:(k + 1) * P], XT[:, 4 * (i % 2) + k, i // 2 * P:(i // 2 + 1) * P],
                                     IDENT)
                m.then_inc(*mark("out_turned", i))

        @block.scalar
        def _(act):
            stage = [0]

            def stage_end():
                stage[0] += 1
                act.drain().then_inc(*mark("stage_end", ("act", stage[0])))
                act.wait_ge(sems["stage_end"], 3 * stage[0])

            def split(c):
                nk = CHUNKS[c][3]
                act.wait_ge(*at(f"w_loaded{c % NRAW}", c))
                if c >= NSPLIT:
                    act.wait_ge(*at("w_used", c - NSPLIT))
                nc.scalar.activation(WH[:, c % NSPLIT, 0:nk, :], RAW[:, c % NRAW, 0:nk, :], ACT.Copy).then_inc(
                    *mark("w_hi", c))

            def split_ahead(c):
                if c + AHEAD < len(CHUNKS):
                    split(c + AHEAD)

            def rows_in():
                act.wait_ge(*at("zeroed", "rows"))
                views = {"b_ada": A["b_ada"].rearrange("l (r p) -> (l r) p", p=P),
                         "conv_w": A["conv_w"].rearrange("l t (r p) -> (l t r) p", p=P),
                         "conv_b": A["conv_b"].rearrange("l (r p) -> (l r) p", p=P),
                         "conv_w_2": A["conv_w_2"].rearrange("l t (r p) -> (l t r) p", p=P),
                         "c": A["c"].rearrange("b (r p) -> (b r) p", p=P),
                         "c_ctx": A["c_ctx"].rearrange("(r p) -> r p", p=P)}
                for name, (c0, n) in PCOL.items():
                    if name == "gains":
                        continue
                    v = views[name] if name in views else A[name].rearrange("l (r p) -> (l r) p", p=P)
                    a = c0
                    while a < c0 + n:
                        b = min(c0 + n, (a // P + 1) * P)
                        act.dma_start(PROWS[a % P:a % P + b - a, a // P, :], v[a - c0:b - c0, :]).then_inc(
                            *mark("rows_in", (name, a), 16))
                        a = b
                for l in range(DEPTH):
                    for i, name in enumerate(GAINS):
                        c = PCOL["gains"][0] + l * 6 + i
                        w = A[name].shape[1]
                        for r in range(P // w):
                            act.dma_start(PROWS[c % P:c % P + 1, c // P, r * w:(r + 1) * w], A[name][l:l + 1, :]).then_inc(
                                *mark("rows_in", "last" if (l, i, r) == (DEPTH - 1, 5, P // w - 1) else (name, l, r), 16))
                act.dma_start(RPBR[:, 48:79], A["rpb_b"].rearrange("l h a b -> (l h a) b")).then_inc(
                    *mark("bias_in", "rpb", 16))
                act.dma_start(RELR[:, 127:127 + REL_SIZE], A["rel_reversed"].rearrange("l h r -> (l h) r")).then_inc(
                    *mark("bias_in", "last", 16))

            def norm(S, src, T, bias):
                for k in range(KT):
                    if k >= 2:
                        act.wait_ge(*at("sum_step", (S, max(k - 2, 1))))
                    nc.scalar.activation(SQ[k % 2][:, 0:T], src[:, k, 0:T], ACT.Square).then_inc(
                        *mark("sq_ready", (S, k)))
                act.wait_ge(*at("stat_done", S))
                nc.scalar.activation(RSTD[:, 0:T], PS[:, 0, 0:T], ACT.Sqrt, bias=EPSC[:, 0:1]).then_inc(
                    *mark("std_ready", S))
                for k in range(KT):
                    act.wait_ge(*at("norm_mid", (S, k)))
                    nc.scalar.activation(HH[:, k, 0:T], TMP[k % 2][:, 0:T], ACT.Identity, bias=bias(k)).then_inc(
                        *mark("h_hi", (S, k)))
                stage_end()

            def project(S, tiles, c0, T, dst, off, beside=lambda i: None):
                n = len(tiles)
                for i in range(n + 1):
                    beside(i - 1)
                    if i < n:
                        split_ahead(c0 + i)
                        t = tiles[i]
                        ps = PS[:, lin_bank(i), 0:T]
                        act.wait_ge(*at("w_used", c0 + i))
                        if "blk" in t or is_value(t):
                            p = aux_before(tiles, i)
                            if p is not None:
                                act.wait_ge(*at("v_turned" if is_value(tiles[p]) else "blk_done", (S, p)))
                        if "blk" in t:
                            nc.scalar.activation(SQ[i % 2][:, 0:T], ps, ACT.Square).then_inc(
                                *mark("raw_squared", (S, i)))
                        to = SQ[i % 2][:, 0:T] if is_value(t) else dst[:, t["slot"], off:off + T]
                        nc.scalar.activation(to, ps, ACT.Copy, scale=t.get("scale", 1.0)).then_inc(
                            *mark("raw_copied", (S, i)))
                    j = i - 1
                    if 0 <= j < n and "blk" in tiles[j]:
                        act.wait_ge(*at("blk_done", (S, j)))
                        if j >= 2 and "blk" in tiles[j - 2]:
                            act.wait_ge(*at("qk_step", (S, j - 2, "norm")))
                        nc.scalar.activation(TMP[j % 2][:, 0:T], PS[:, 4 + j % 2, 0:T], ACT.Sqrt,
                                             bias=EPSC[:, 0:1], scale=1.0 / (64, 32)[tiles[j]["blk"]]).then_inc(
                                                 *mark("blk_std", (S, j)))

            def out_proj(c0):
                for n in range(KT):
                    split_ahead(c0 + n)

            def attend(att):
                S, units, groups, PTt = att["S"], att["units"], att["groups"], att["PT"]
                owner = {s: u for u, unit in enumerate(units) for s in unit["sub"]}
                lag, nprob = att["lag"], len(att["prob"])
                for i in range(len(units) + lag + 4):
                    if i < len(units):
                        u = units[i]
                        for m, s in enumerate(u["sub"]):
                            act.wait_ge(*at("neg_max", (S, s)))
                            if s >= nprob:
                                o = owner[s - nprob]
                                act.wait_ge(*(at("mix_step", (S, o, "mixed")) if s - nprob != units[o]["sub"][-1] else
                                              at("probs_turned_b" if att["wide"] else "probs_turned_a", (S, o))))
                            if u["head"] == 0 and u["group"] >= NSUM:
                                act.wait_ge(*at("o_step", (S, u["group"] - NSUM, "scaled")))
                            nc.scalar.activation(
                                att["prob"][s % nprob][:, 0:u["nk"]], scores(att, s)[:, 0:u["nk"]],
                                ACT.Exp, bias=NMAX[:, s % 4:s % 4 + 1],
                                accum_out=SUMS[:, u["group"] % NSUM, 8 * m + u["head"]:8 * m + u["head"] + 1]).then_inc(
                                    *mark("exp_done", (S, s)))
                    j = i - lag
                    if 0 <= j < len(units):
                        u = units[j]
                        w = min(u["nk"], 512)
                        act.wait_ge(*at("probs_turned_a", (S, j)))
                        if j >= 2:
                            act.wait_ge(*at("pv_done", (S, j - 2)))
                        nc.scalar.activation(PTt[:, j % 2, 0:w], PS[:, turn_bank(att, j), 0:w], ACT.Copy).then_inc(
                            *mark("pt_copied_a", (S, j)))
                    j = i - lag - 2
                    if 0 <= j < len(units) and units[j]["last"] and groups[units[j]["group"]]["diff"]:
                        g = units[j]["group"]
                        act.wait_ge(*at("o_step", (S, g, "ss")))
                        nc.scalar.activation(SSQ[:, 1, :], SSQ[:, 0, :], ACT.Sqrt, bias=EPSC[:, 0:1],
                                             scale=1.0 / HEAD).then_inc(*mark("sub_std", (S, g)))
                    j = i - lag - 3
                    if 0 <= j < len(units) and units[j].get("tile_last"):
                        t, f = units[j]["t"], att["first"]
                        for part, bank, a, b in (("a", 4, 0, 4), ("b", 5, 4, att["tiles"])):
                            act.wait_ge(*at(f"o_turned_{part}", (S, t)))
                            nc.scalar.activation(HH[:, f + a:f + b, t * P:(t + 1) * P],
                                                 PS[:, bank, 0:(b - a) * P].rearrange("p (k c) -> p k c", c=P),
                                                 ACT.Copy).then_inc(*mark("o_hi", (S, t, part)))

            def ffn(S, c0, T, l, groups, parts):
                total = sum(n for _, n in groups)
                place = [(g, j) for g, (_, n) in enumerate(groups) for j in range(n)]
                downs = {}
                steps = ffn_steps(groups, parts)
                for n, step in enumerate(steps):
                    if step[0] == "down":
                        downs[step[1]] = c0 + n

                def silu(q):
                    act.wait_ge(*at("conv_step", (S, 2 * q + 1, "after")))
                    nc.scalar.activation(MG[:, q % 3, 0:T], MG[:, q % 3, 0:T], ACT.Silu).then_inc(
                        *mark("silu_ready", (S, q)))

                def hidden_hi(q):
                    g, j = place[q]
                    act.wait_ge(*at("prod_ready", (S, q)))
                    if g >= 2 and j == 0:
                        act.wait_ge(*at("w_used", downs[g - 2]))
                    nc.scalar.activation(GH[:, g % 2, j, 0:T], MG[:, q % 3, 0:T], ACT.Copy).then_inc(
                        *mark("hid_hi", (S, q)))

                up = 0
                for n, step in enumerate(steps):
                    split_ahead(c0 + n)
                    if step[0] == "down":
                        continue
                    q, part = up // parts, up % parts
                    act.wait_ge(*at("w_used", c0 + n))
                    if q >= 3:
                        act.wait_ge(*at("hid_lo", (S, q - 3)))
                    if parts == 2:
                        i = part * FT + q
                        nc.scalar.activation((MU, MG)[part][:, q % 3, 0:T], PS[:, lin_bank(up), 0:T], ACT.Identity,
                                             bias=prm("conv_b", l * 2 * FT + i),
                                             scale=prm("conv_w", l * 6 * FT + 2 * FT + i)).then_inc(
                                                 *mark("mid_ready", (S, up)))
                        if part == 1:
                            if q >= 1:
                                silu(q - 1)
                            if q >= 2:
                                hidden_hi(q - 2)
                            if q == total - 1:
                                silu(q)
                                hidden_hi(q - 1)
                                hidden_hi(q)
                    else:
                        nc.scalar.activation(MU[:, q % 3, 0:T], PS[:, lin_bank(up), 0:T], ACT.Relu).then_inc(
                            *mark("mid_ready", (S, up)))
                        if q >= 1:
                            hidden_hi(q - 1)
                        if q == total - 1:
                            hidden_hi(q)
                    up += 1

            def layer_norm(S, c0=None):
                if c0 is not None:
                    split_ahead(c0)
                for k in range(KT):
                    if k == 2 and c0 is not None:
                        split_ahead(c0 + 1)
                    act.wait_ge(*at("norm_step", (S, k)))
                    if k >= 2:
                        act.wait_ge(*at("sum_step", ((S, "var"), max(k - 2, 1))))
                    nc.scalar.activation(SQ[k % 2], XT[:, k, :], ACT.Square).then_inc(*mark("sq_ready", (S, k)))
                act.wait_ge(*at("stat_done", (S, "var")))
                nc.scalar.activation(RSTD[:, :], PS[:, 7, :], ACT.Sqrt, bias=EPSC[:, 1:2]).then_inc(
                    *mark("std_ready", S))
                if c0 is not None:
                    split_ahead(c0 + 2)
                name = S[0]
                for k in range(KT):
                    act.wait_ge(*at("norm_mid", (S, k)))
                    nc.scalar.activation(XT[:, k, :], TMP[k % 2], ACT.Identity,
                                         bias=prm(name + "_b_2", S[1] * KT + k)).then_inc(*mark("x_ready", (S, k)))
                    act.wait_ge(*at("x_ready", (S, k)))
                    nc.scalar.activation(HH[:, k, :], XT[:, k, :], ACT.Copy).then_inc(*mark("h_hi", (S, k)))
                stage_end()

            act.dma_start(PACK[:, :], A["const_pack"]).then_inc(*mark("consts_in", "pack", 16))
            for i, name in enumerate(("lambda_q1", "lambda_k1", "lambda_q2", "lambda_k2")):
                for l in range(DEPTH):
                    act.dma_start(LAMV[:, l, i, :], A[name][l:l + 1, :].broadcast_to([P, 32])).then_inc(
                        *mark("consts_in", (name, l), 16))
            for l in range(DEPTH):
                act.dma_start(GSUB[:, l, :], A["g_subln"][l:l + 1, :].broadcast_to([P, HEAD])).then_inc(
                    *mark("consts_in", ("g_sub", l), 16))
            act.dma_start(RELC[:, :], bass.AP(A["rel_reversed"].tensor, 0, [[0, P], [REL_SIZE, 12]]),
                          allow_slow_non_contiguous=True).then_inc(*mark("consts_in", "last", 16))
            rows_in()
            for i in range(6):
                src = A["x"][0, i * P:(i + 1) * P, :] if i < 4 else A["ctx"][0, (i - 4) * P:(i - 3) * P, :]
                act.dma_start(XN[:, i, :], src).then_inc(*mark("acts_in", "last" if i == 5 else i, 16))
            act.wait_ge(*at("zeroed", "rel"))
            act.dma_start(RPB_PAD, RPBR[:, :].unsqueeze(1).broadcast_to([120, 64, P])).then_inc(
                *mark("pad_written", "rpb", 16))
            act.dma_start(REL_PAD, RELR[:, :].unsqueeze(1).broadcast_to([12, P, 384])).then_inc(
                *mark("pad_written", "last", 16))
            act.wait_ge(*at("turned_taken", "params"))
            c0 = PCOL["c"][0] % P
            silu_in = PRM[:, PCOL["c"][0] // P, c0:c0 + 16].rearrange("p (s k) -> p k s", s=2)
            nc.scalar.activation(SILU[:, :, :], silu_in, ACT.Silu).then_inc(*mark("param_act", "silu"))
            act.wait_ge(*at("param_step", "lam_sum"))
            nc.scalar.activation(LAM[:, :, 0:2], LAM[:, :, 2:4], ACT.Exp).then_inc(*mark("param_act", "lam_exp"))
            for c in range(AHEAD):
                split(FIRST["qkv", "c", 0] + c)
            stage_end()
            for l in range(DEPTH):
                for i in range(4):
                    act.dma_start(ROPE[:, i, :], A["const_rope"][:, i, :]).then_inc(
                        *mark("tab_in", ("rope", l) if i == 3 else (l, i), 16))
                act.wait_ge(*at("pad_written", "last"))
                for part in range(2):
                    for h in range(B_HEADS):
                        row = (l * B_HEADS + h) * 15 + 1 - part
                        act.dma_start(TB[64 * part:64 * part + 64, h, :, :],
                                      bass.AP(RPB_PAD.tensor, row * 64 * P + 63, [[P - 1, 64], [64 * P, 14], [1, 64]])
                                      ).then_inc(*mark("tab_in", ("win", l) if (part, h) == (1, 3) else (l, part, "w", h), 16))
                for s in ("c", "x"):
                    norm(("n1", s, l), XT if s == "x" else CT, TOKENS[s],
                         lambda k: MOD[:, l, k, int(s == "c"):int(s == "c") + 1])
                    project(("qkv", s, l), qkv_tiles(s, l), FIRST["qkv", s, l], TOKENS[s], QK, SEQ if s == "c" else 0)
                    stage_end()
                for s in streams(l):
                    attend(number_attention(("att", s, l), attention_units_1(s, l)))
                    stage_end()
                    out_proj(FIRST["out", s, l])
                    stage_end()
                for s in streams(l):
                    norm(("n2", s, l), XT if s == "x" else CT, TOKENS[s],
                         lambda k: MOD[:, l, 24 + k, int(s == "c"):int(s == "c") + 1])
                    ffn(("ffn", s, l), FIRST["ffn", s, l], TOKENS[s], l, GROUPS_1, 2)
                    stage_end()
            for i in range(2):
                act.dma_start(XN[:, i, :], A["mem_2"][0, i * P:(i + 1) * P, :]).then_inc(
                    *mark("mem_in", "last" if i else 0, 16))
            for k in range(KT):
                nc.scalar.activation(HH[:, k, :], XT[:, k, :], ACT.Copy).then_inc(*mark("h_hi", ("x", k)))
            stage_end()
            for l in range(DEPTH):
                if l == 0:
                    act.dma_start(POSI[:, :], A["positions_2"][0:1, :].broadcast_to([P, SEQ])).then_inc(
                        *mark("tab_in", ("pos", l), 16))
                for h in range(6):
                    act.dma_start(TBK[:, h, :], bass.AP(REL_PAD.tensor, (l * 6 + h) * P * 384 + 127, [[383, P], [1, 256]])
                                  ).then_inc(*mark("bias2_in", (l, h), 16))
                def sines(tables):
                    for i in tables:
                        act.wait_ge(*at("trig_step", (l, i, "max")))
                        nc.scalar.activation(ROPE2[:, i, :], ROPE2[:, i, :], ACT.Sin).then_inc(*mark("trig_act", (l, i)))

                def beside(step):
                    if step == 2 and l == 0:
                        sines((0, 1))
                    for n in index_logits(step):
                        t = INDEX_STEPS[n][0]
                        act.wait_ge(*at("idx_done", (l, n)))
                        if n >= 2:
                            act.wait_ge(*at("idx_step", (l, n - 2)))
                        nc.scalar.activation(TMP[n % 2][:, 0:(t + 1) * P], PS[:, 4 + n % 2, 0:(t + 1) * P],
                                             ACT.Relu).then_inc(*mark("idx_relu", (l, n)))

                if l == 0:
                    sines((2, 3))
                project(("mix_in", l), mixer_tiles(), FIRST["mix_in", l], SEQ, QK2, 0, beside)
                stage_end()
                for m in range(2):
                    nc.scalar.activation(HH[:, m, :], QK2[:, 17 + m, :], ACT.Copy).then_inc(*mark("cv_hi", (l, m)))
                attend(number_attention(("att2", l), attention_units_2(l)))
                stage_end()
                kv = ("mem_kv", l)
                nc.scalar.activation(MH[:, :, :], CT[:, :, :], ACT.Copy).then_inc(*mark("mem_hi_made", l))
                out_proj(FIRST["mix_out", l])
                stage_end()
                layer_norm(("ln1", l), FIRST[kv])
                for n in range(2 * KT):
                    if n >= 3:
                        split_ahead(FIRST[kv] + n)
                    act.wait_ge(*at("w_used", FIRST[kv] + n))
                    if n >= KT + 2:
                        act.wait_ge(*at("v_turned", (kv, n - 2)))
                    nc.scalar.activation(MK[:, n, :] if n < KT else SQ[n % 2][:, 0:MEM], PS[:, lin_bank(n), 0:MEM],
                                         ACT.Copy).then_inc(*mark("raw_copied", (kv, n)))
                for n in range(KT):
                    split_ahead(FIRST["mem_q", l] + n)
                    act.wait_ge(*at("w_used", FIRST["mem_q", l] + n))
                    nc.scalar.activation(MQ[:, n, :], PS[:, lin_bank(n), :], ACT.Copy, scale=1.0 / 16).then_inc(
                        *mark("raw_copied", (("mem_q", l), n)))
                stage_end()
                attend(number_attention(("att3", l), attention_units_3()))
                stage_end()
                out_proj(FIRST["mem_out", l])
                stage_end()
                layer_norm(("ln2", l))
                ffn(("ff", l), FIRST["ff", l], SEQ, l, GROUPS_2, 1)
                stage_end()
                layer_norm(("ln3", l))
            for i in range(8):
                act.wait_ge(*at("out_turned", i))
                nc.scalar.activation(OUTS[:, i // 2, 512 * (i % 2):512 * (i % 2) + 512], PS[:, i, :], ACT.Copy).then_inc(
                    *mark("out_copied", i))
                if i % 2:
                    act.wait_ge(*at("out_copied", i))
                    act.dma_start(out[0, i // 2 * P:(i // 2 + 1) * P, :], OUTS[:, i // 2, :]).then_inc(
                        *mark("out_stored", i, 16))
            act.wait_ge(*at("out_stored", 7))

        @block.vector
        def _(dve):
            stage = [0]

            def stage_end():
                stage[0] += 1
                dve.drain().then_inc(*mark("stage_end", ("dve", stage[0])))
                dve.wait_ge(sems["stage_end"], 3 * stage[0])

            def own(name, key, ins):
                ins.then_inc(*mark(name, key))
                dve.wait_ge(*at(name, key))

            def lo(name, key, out_ap, full, hi):
                nc.vector.tensor_tensor(out_ap, full, hi.bitcast(F32), ALU.subtract).then_inc(*mark(name, key))

            def add_up(S, tile, wait, T):
                for k in range(1, KT):
                    for m in ((0, 1) if k == 1 else (k,)):
                        wait(m)
                    a = tile(0) if k == 1 else ACC[:, 0:T]
                    nc.vector.tensor_tensor(ACC[:, 0:T], a, tile(k), ALU.add).then_inc(
                        *mark("sum_step", (S, "total" if k == KT - 1 else k)))
                    dve.wait_ge(*at("sum_step", (S, "total" if k == KT - 1 else k)))

            def turn_in(S, n, dst):
                for i in range(n):
                    for half in range(2):
                        dve.wait_ge(*at("turned", (S, 2 * i + half)))
                        d, t = dst(i)
                        nc.vector.tensor_copy(d[:, 4 * half:4 * half + 4, t * P:(t + 1) * P],
                                              PS[:, (2 * i + half) % 8, :].rearrange("p (k c) -> p k c", c=P)).then_inc(
                                                  *mark("turned_taken", (S, 2 * i + half)))

            def norm(S, src, T, gain, bias):
                add_up(S, lambda k: SQ[k % 2][:, 0:T], lambda k: dve.wait_ge(*at("sq_ready", (S, k))), T)
                dve.wait_ge(*at("std_ready", S))
                own("norm_step", (S, "recip"), nc.vector.reciprocal(RSTD[:, 0:T], RSTD[:, 0:T]))
                for k in range(KT + 1):
                    if k < KT:
                        if k >= 2:
                            dve.wait_ge(*at("h_lo", (S, k - 2)))
                        nc.vector.scalar_tensor_tensor(TMP[k % 2][:, 0:T], src[:, k, 0:T], gain(k), RSTD[:, 0:T],
                                                       ALU.mult, ALU.mult).then_inc(*mark("norm_mid", (S, k)))
                    if k:
                        j = k - 1
                        dve.wait_ge(*at("h_hi", (S, j)))
                        nc.vector.scalar_tensor_tensor(HL[:, j, 0:T], TMP[j % 2][:, 0:T], bias(j),
                                                       HH[:, j, 0:T].bitcast(F32), ALU.add, ALU.subtract).then_inc(
                                                           *mark("h_lo", (S, j)))
                stage_end()

            def project(S, tiles, c0, T, dst, off, tables, v_dst, beside=lambda i: None):
                n = len(tiles)
                rotated = []
                for i in range(n + 2):
                    beside(i - 1)
                    j = i - 1
                    if 0 <= j < n and "blk" in tiles[j]:
                        t = tiles[j]
                        q = dst[:, t["slot"], off:off + T]
                        r = TMP[j % 2][:, 0:T]
                        dve.wait_ge(*at("blk_std", (S, j)))
                        own("qk_step", (S, j, "recip"), nc.vector.reciprocal(r, r))
                        dve.wait_ge(*at("raw_copied", (S, j)))
                        nc.vector.scalar_tensor_tensor(q, q, HG[:, S[2], t["gain"]:t["gain"] + 1], r, ALU.mult,
                                                       ALU.mult).then_inc(*mark("qk_step", (S, j, "norm")))
                    j = i - 2
                    if 0 <= j < n and tiles[j]["kind"] == "qk" and tiles[j]["rope"] is not None:
                        t = tiles[j]
                        q = dst[:, t["slot"], off:off + T]
                        r = (ACC, RSTD)[j % 2][:, 0:T]
                        dve.wait_ge(*at("rot_done", (S, j)))
                        prev = [m for m in rotated if m % 2 == j % 2]
                        if prev:
                            dve.wait_ge(*at("rope_step", (S, prev[-1], "sum")))
                        rotated.append(j)
                        if S[0] == "mix_in":
                            dve.wait_ge(*at("trig_act", (0, t["rope"] + 1)))
                        nc.vector.tensor_tensor(r, PS[:, 6 + j % 2, 0:T], tables[:, t["rope"] + 1, 0:T], ALU.mult).then_inc(
                            *mark("rope_step", (S, j, "sin")))
                        own("rope_step", (S, j, "cos"), nc.vector.tensor_tensor(q, q, tables[:, t["rope"], 0:T], ALU.mult))
                        nc.vector.tensor_tensor(q, q, r, ALU.add).then_inc(*mark("rope_step", (S, j, "sum")))
                    j = i - 1
                    if 0 <= j < n and is_value(tiles[j]):
                        dve.wait_ge(*at("v_turned", (S, j)))
                        nc.vector.tensor_copy(v_dst(tiles[j]), PS[:, 4 + j % 2, 0:T].rearrange("p (t c) -> p t c", c=P)
                                              ).then_inc(*mark("v_copied", (S, j)))

            def residual(S, n, c, ps, k, T, x, gate, scale, prev=None, mean=None):
                dve.wait_ge(*at("w_used", c))
                if prev is not None:
                    dve.wait_ge(*at("resid", prev))
                if gate is not None:
                    i = nc.vector.scalar_tensor_tensor(x[:, k, 0:T], ps, gate, x[:, k, 0:T], ALU.mult, ALU.add)
                else:
                    i = nc.vector.scalar_tensor_tensor(x[:, k, 0:T], x[:, k, 0:T], scale, ps, ALU.mult, ALU.add)
                i.then_inc(*mark("resid", (S, n)))
                if mean is not None and k:
                    key = (mean, "mean"), "total" if k == KT - 1 else k
                    dve.wait_ge(*at("resid", (S, n)))
                    nc.vector.tensor_tensor(ACC[:, :], x[:, 0, :] if k == 1 else ACC[:, :], x[:, k, :], ALU.add).then_inc(
                        *mark("sum_step", key))
                    dve.wait_ge(*at("sum_step", key))

            def out_proj(S, c0, T, x, gate, mean=None):
                for n in range(KT):
                    residual(S, n, c0 + n, PS[:, lin_bank(n), 0:T], n, T, x, gate(n), ALPHA, mean=mean)

            def attend(att):
                S, units, groups, PTt, ONt = att["S"], att["units"], att["groups"], att["PT"], att["ON"]
                lag, prob = att["lag"], att["prob"]
                for i in range(len(units) + lag + 4):
                    j = i - 1
                    if 0 <= j < len(units) and len(units[j]["sub"]) == 2:
                        g, h, nk = (units[j][key] for key in ("group", "head", "nk"))
                        s0, s1 = units[j]["sub"]
                        p0, p1 = (prob[s % len(prob)][:, 0:nk] for s in (s0, s1))
                        dve.wait_ge(*at("exp_done", (S, s1)))
                        own("mix_step", (S, j, "recip"),
                            nc.vector.reciprocal(COEF[:, 0:1], SUMS[:, g % NSUM, 8 + h:9 + h]))
                        own("mix_step", (S, j, "coef"),
                            nc.vector.tensor_scalar(COEF[:, 1:2], SUMS[:, g % NSUM, h:h + 1], COEF[:, 0:1],
                                                    LAM[:, groups[g]["layer"], 2:3], ALU.mult, ALU.mult))
                        own("mix_step", (S, j, "mixed"),
                            nc.vector.scalar_tensor_tensor(p1, p1, COEF[:, 1:2], p0, ALU.mult, ALU.add))
                    if i < len(units):
                        u = units[i]
                        for s in u["sub"]:
                            ps = scores(att, s)
                            dve.wait_ge(*at("scores_done", (S, s)))
                            for n, (a, b, bias) in enumerate(u["adds"]):
                                if bias.shape[1] == 1:
                                    ins = nc.vector.tensor_scalar(ps[:, a:b], ps[:, a:b], bias, None, ALU.add)
                                else:
                                    ins = nc.vector.tensor_tensor(ps[:, a:b], ps[:, a:b], bias, ALU.add)
                                own("bias_step", (S, s, n), ins)
                            nc.vector.tensor_reduce(NMAX[:, s % 4:s % 4 + 1], ps[:, 0:u["nk"]], AX.X, ALU.max,
                                                    negate=True).then_inc(*mark("neg_max", (S, s)))
                    j = i - lag
                    if 0 <= j < len(units):
                        nk = units[j]["nk"]
                        if nk > 512:
                            dve.wait_ge(*at("probs_turned_b", (S, j)))
                            if j >= 2:
                                dve.wait_ge(*at("pv_done", (S, j - 2)))
                            nc.vector.tensor_copy(PTt[:, j % 2, 512:nk], PS[:, 5, 0:nk - 512]).then_inc(
                                *mark("pt_copied_b", (S, j)))
                    j = i - lag - 2
                    if 0 <= j < len(units) and units[j]["last"]:
                        u = units[j]
                        g, t = u["group"], u["t"]
                        gr = groups[g]
                        nh, dv = gr["heads"], gr["dv"]
                        on = ONt[:, t % 2, gr["col"]:gr["col"] + nh * dv].rearrange("p (h d) -> p h d", d=dv)
                        dve.wait_ge(*at("pv_done", (S, j)))
                        if t >= 2:
                            dve.wait_ge(*at("o_turned_b", (S, t - 2)))
                        own("o_step", (S, g, "recip"), nc.vector.reciprocal(RSUM[:, g % 2, 0:nh], SUMS[:, g % NSUM, 0:nh]))
                        own("o_step", (S, g, "scaled"),
                            nc.vector.tensor_tensor(on, PS[:, 6 + g % 2, 0:nh * dv].rearrange("p (h d) -> p h d", d=dv),
                                                    RSUM[:, g % 2, 0:nh].unsqueeze(2).broadcast_to([P, nh, dv]), ALU.mult))
                        if gr["diff"]:
                            sq = ACC[:, 0:nh * dv].rearrange("p (h d) -> p h d", d=dv)
                            own("o_step", (S, g, "sq"), nc.vector.tensor_tensor(sq, on, on, ALU.mult))
                            nc.vector.tensor_reduce(SSQ[:, 0, :], sq, AX.X, ALU.add).then_inc(
                                *mark("o_step", (S, g, "ss")))
                    j = i - lag - 3
                    if 0 <= j < len(units) and units[j]["last"] and groups[units[j]["group"]]["diff"]:
                        u = units[j]
                        g, t = u["group"], u["t"]
                        gr = groups[g]
                        nh, dv = gr["heads"], gr["dv"]
                        on = ONt[:, t % 2, gr["col"]:gr["col"] + nh * dv].rearrange("p (h d) -> p h d", d=dv)
                        dve.wait_ge(*at("sub_std", (S, g)))
                        own("o_step", (S, g, "rstd"), nc.vector.reciprocal(SSQ[:, 1, :], SSQ[:, 1, :]))
                        own("o_step", (S, g, "normed"),
                            nc.vector.tensor_tensor(on, on, SSQ[:, 1, :].unsqueeze(2).broadcast_to([P, nh, dv]), ALU.mult))
                        nc.vector.tensor_tensor(on, on, GSUB[:, gr["layer"], :].unsqueeze(1).broadcast_to([P, nh, dv]),
                                                ALU.mult).then_inc(*mark("o_step", (S, g, "ready")))
                    if 0 <= j < len(units) and units[j].get("tile_last"):
                        t, f = units[j]["t"], att["first"]
                        for part, bank, a, b in (("a", 4, 0, 4), ("b", 5, 4, att["tiles"])):
                            dve.wait_ge(*at("o_hi", (S, t, part)))
                            lo("o_lo", (S, t, part), HL[:, f + a:f + b, t * P:(t + 1) * P],
                               PS[:, bank, 0:(b - a) * P].rearrange("p (k c) -> p k c", c=P),
                               HH[:, f + a:f + b, t * P:(t + 1) * P])

            def ffn(S, c0, T, l, groups, parts, x, gate, mean=None):
                total = sum(n for _, n in groups)
                place = [(g, j) for g, (_, n) in enumerate(groups) for j in range(n)]

                def product(q):
                    if parts == 2:
                        dve.wait_ge(*at("silu_ready", (S, q)))
                        nc.vector.tensor_tensor(MG[:, q % 3, 0:T], MG[:, q % 3, 0:T], MU[:, q % 3, 0:T],
                                                ALU.mult).then_inc(*mark("prod_ready", (S, q)))
                    else:
                        dve.wait_ge(*at("mid_ready", (S, q)))
                        if q >= 3:
                            dve.wait_ge(*at("hid_lo", (S, q - 3)))
                        nc.vector.tensor_tensor(MG[:, q % 3, 0:T], MU[:, q % 3, 0:T], MU[:, q % 3, 0:T],
                                                ALU.mult).then_inc(*mark("prod_ready", (S, q)))

                def hidden_lo(q):
                    g, j = place[q]
                    dve.wait_ge(*at("hid_hi", (S, q)))
                    lo("hid_lo", (S, q), GL[:, g % 2, j, 0:T], MG[:, q % 3, 0:T], GH[:, g % 2, j, 0:T])

                up = down = 0
                for n, step in enumerate(ffn_steps(groups, parts)):
                    if step[0] == "down":
                        _, g, k = step
                        residual(S, down, c0 + n, PS[:, 4 + down % 4, 0:T], k, T, x, gate(k), ALPHA if g == 0 else 1.0,
                                 (S, down - KT) if down >= KT else None, mean if g == len(groups) - 1 else None)
                        down += 1
                        continue
                    q, part = up // parts, up % parts
                    if parts == 2:
                        i = l * 6 * FT + part * FT + q
                        m = (MU, MG)[part]
                        ps = PS[:, lin_bank(up), 0:T]
                        dve.wait_ge(*at("mid_ready", (S, up)))
                        own("conv_step", (S, up, "before"), nc.vector.scalar_tensor_tensor(
                            m[:, q % 3, 1:T], ps[:, 0:T - 1], prm("conv_w", i), m[:, q % 3, 1:T], ALU.mult, ALU.add))
                        nc.vector.scalar_tensor_tensor(
                            m[:, q % 3, 0:T - 1], ps[:, 1:T], prm("conv_w", i + 4 * FT), m[:, q % 3, 0:T - 1],
                            ALU.mult, ALU.add).then_inc(*mark("conv_step", (S, up, "after")))
                        if part == 1:
                            if q >= 1:
                                product(q - 1)
                            if q >= 2:
                                hidden_lo(q - 2)
                            if q == total - 1:
                                product(q)
                                hidden_lo(q - 1)
                                hidden_lo(q)
                    else:
                        product(q)
                        if q >= 1:
                            hidden_lo(q - 1)
                        if q == total - 1:
                            hidden_lo(q)
                    up += 1

            def layer_norm(S):
                dve.wait_ge(*at("stat_done", (S, "mean")))
                for k in range(KT):
                    nc.vector.tensor_tensor(XT[:, k, :], XT[:, k, :], PS[:, 6, :], ALU.subtract).then_inc(
                        *mark("norm_step", (S, k)))
                add_up((S, "var"), lambda k: SQ[k % 2], lambda k: dve.wait_ge(*at("sq_ready", (S, k))), SEQ)
                dve.wait_ge(*at("std_ready", S))
                own("norm_step", (S, "recip"), nc.vector.reciprocal(RSTD[:, :], RSTD[:, :]))
                for k in range(KT + 1):
                    if k < KT:
                        if k >= 2:
                            dve.wait_ge(*at("x_ready", (S, k - 2)))
                        nc.vector.scalar_tensor_tensor(TMP[k % 2], XT[:, k, :], prm(S[0] + "_g_2", S[1] * KT + k),
                                                       RSTD[:, :], ALU.mult, ALU.mult).then_inc(*mark("norm_mid", (S, k)))
                    if k:
                        dve.wait_ge(*at("h_hi", (S, k - 1)))
                        lo("h_lo", (S, k - 1), HL[:, k - 1, :], XT[:, k - 1, :], HH[:, k - 1, :])
                stage_end()

            nc.vector.memset(PROWS[:, NGRP - 1, :], 0.0).then_inc(*mark("zeroed", "prows"))
            nc.vector.memset(RPBR[:, :], 0.0).then_inc(*mark("zeroed", "rpb"))
            nc.vector.memset(RELR[:, :], 0.0).then_inc(*mark("zeroed", "rows"))
            nc.vector.memset(EPSC[:, 0:1], EPS).then_inc(*mark("zeroed", "eps"))
            nc.vector.memset(EPSC[:, 1:2], LN_EPS).then_inc(*mark("zeroed", "ln_eps"))
            dve.wait_ge(*at("bias_in", "last"))
            nc.vector.tensor_scalar(RELR[:, 0:127], RELR[:, 0:127], RELR[:, 127:128], None, ALU.add).then_inc(
                *mark("zeroed", "rel"))
            dve.wait_ge(*at("turned", "params"))
            nc.vector.tensor_copy(PRM[:, 0:4, :], PS[:, 6, :].rearrange("p (g c) -> p g c", c=P)).then_inc(
                *mark("param_step", "prm"))
            nc.vector.tensor_copy(PRM[:, 4:NGRP, :], PS[:, 7, 0:(NGRP - 4) * P].rearrange("p (g c) -> p g c", c=P)).then_inc(
                *mark("turned_taken", "params"))
            dve.wait_ge(*at("turned_taken", "params"))
            dve.wait_ge(*at("param_step", "prm"))
            for i, scale in enumerate((0.125, 1.0, 0.125, 1.0, 32.0 ** -0.5, 1.0)):
                src = prm_range("gains", 0, 12).rearrange("p (l i) -> p l i", i=6)[:, :, i]
                nc.vector.tensor_scalar(HG[:, :, i], src, scale, None, ALU.mult).then_inc(*mark("param_step", ("hg", i)))
            prod = ACC[:, 0:128].rearrange("p (l a d) -> p l a d", l=2, a=2)
            for l in range(DEPTH):
                v = LAMV[:, l, :, :].rearrange("p (a b) d -> p a b d", b=2)
                own("param_step", ("lam_prod", l), nc.vector.tensor_tensor(prod[:, l], v[:, :, 0, :], v[:, :, 1, :], ALU.mult))
                nc.vector.tensor_reduce(LAM[:, l, 2:4], prod[:, l], AX.X, ALU.add).then_inc(
                    *mark("param_step", "lam_sum" if l else ("lam_sum", l)))
            dve.wait_ge(*at("param_act", "lam_exp"))
            for l in range(DEPTH):
                lam_init = 0.8 - 0.6 * math.exp(-0.3 * l)
                own("param_step", ("lam_diff", l), nc.vector.tensor_tensor(LAM[:, l, 3:4], LAM[:, l, 1:2], LAM[:, l, 0:1],
                                                                          ALU.subtract))
                own("param_step", ("neg_lam", l), nc.vector.tensor_scalar(LAM[:, l, 2:3], LAM[:, l, 3:4], -lam_init, None,
                                                                         ALU.add))
                nc.vector.tensor_scalar(GSUB[:, l, :], GSUB[:, l, :], 1.0 - lam_init, None, ALU.mult).then_inc(
                    *mark("param_step", ("g_sub", l)))
            for b in range(24):
                dve.wait_ge(*at("w_used", FIRST["ada", 0] + 4 * b + 3))
                nc.vector.tensor_copy(MROW[:, b * 512:(b + 1) * 512], PS[0:2, b % 8, :]).then_inc(*mark("mod_rows", b))
            dve.wait_ge(*at("turned", "mod"))
            for l in range(DEPTH):
                own("param_step", ("mod", l), nc.vector.tensor_tensor(
                    MOD[:, l, :, :], PS[:, l, 0:96].rearrange("p (n s) -> p n s", s=2),
                    prm_range("b_ada", l * 48, 48).unsqueeze(2).broadcast_to([P, 48, 2]), ALU.add))
                for w, name in enumerate(("g_norm1", "g_norm2")):
                    for s in range(2):
                        nc.vector.scalar_tensor_tensor(GMOD[:, l, w, s, :], MOD[:, l, 8 + 24 * w:16 + 24 * w, s], 1.0,
                                                       prm_range(name, l * KT, KT), ALU.add, ALU.mult).then_inc(
                                                           *mark("param_step", ("gmod", l, w, s)))
            turn_in("in", 6, lambda i: (XT, i) if i < 4 else (CT, i - 4))
            stage_end()
            for l in range(DEPTH):
                for s in ("c", "x"):
                    si = int(s == "c")
                    x = CT if si else XT
                    norm(("n1", s, l), x, TOKENS[s], lambda k: GMOD[:, l, 0, si, k:k + 1],
                         lambda k: MOD[:, l, k, si:si + 1])
                    if si:
                        dve.wait_ge(*at("tab_in", ("win", l)))
                        for h in range(B_HEADS):
                            nc.vector.tensor_tensor(TB[:, h], TB[:, h], WINDOW.unsqueeze(1).broadcast_to([P, 14, 64]),
                                                    ALU.add).then_inc(*mark("bias_step", ("window", l, h)))
                    t0 = 4 if si else 0
                    nt = TOKENS[s] // P
                    project(("qkv", s, l), qkv_tiles(s, l), FIRST["qkv", s, l], TOKENS[s], QK, SEQ if si else 0, ROPE,
                            lambda t: VN[:, t0:t0 + nt, t["col"]:t["col"] + P])
                    stage_end()
                for s in streams(l):
                    si = int(s == "c")
                    attend(number_attention(("att", s, l), attention_units_1(s, l)))
                    stage_end()
                    out_proj(("out", s, l), FIRST["out", s, l], TOKENS[s], CT if si else XT,
                             lambda k: MOD[:, l, 16 + k, si:si + 1])
                    stage_end()
                for s in streams(l):
                    si = int(s == "c")
                    x = CT if si else XT
                    norm(("n2", s, l), x, TOKENS[s], lambda k: GMOD[:, l, 1, si, k:k + 1],
                         lambda k: MOD[:, l, 24 + k, si:si + 1])
                    ffn(("ffn", s, l), FIRST["ffn", s, l], TOKENS[s], l, GROUPS_1, 2, x,
                        lambda k: MOD[:, l, 40 + k, si:si + 1])
                    stage_end()
            for k in range(KT):
                dve.wait_ge(*at("h_hi", ("x", k)))
                lo("h_lo", ("x", k), HL[:, k, :], XT[:, k, :], HH[:, k, :])
            turn_in("mem", 2, lambda i: (CT, i))
            stage_end()
            for l in range(DEPTH):
                def angles(tables):
                    for i in tables:
                        shift = 0.0 if i % 2 else math.pi / 2
                        r = ROPE2[:, i, :]
                        own("trig_step", (l, i, "angle"), nc.vector.tensor_scalar(SQ[0], TMP[0], FREQ[:, i // 2:i // 2 + 1],
                                                                                 None, ALU.mult))
                        own("trig_step", (l, i, "turns"), nc.vector.tensor_scalar(TMP[1], SQ[0], shift, 1.0 / (2 * math.pi),
                                                                                 ALU.add, ALU.mult))
                        own("trig_step", (l, i, "round_up"), nc.vector.tensor_scalar(TMP[1], TMP[1], ROUND, None, ALU.add))
                        own("trig_step", (l, i, "round"), nc.vector.tensor_scalar(TMP[1], TMP[1], ROUND, None, ALU.subtract))
                        for n, part in enumerate(TWO_PI_PARTS):
                            own("trig_step", (l, i, n), nc.vector.scalar_tensor_tensor(
                                r, TMP[1], -part, SQ[0] if n == 0 else r, ALU.mult, ALU.add))
                        own("trig_step", (l, i, "min"), nc.vector.tensor_scalar(r, r, shift, SIN_MAX, ALU.add, ALU.min))
                        own("trig_step", (l, i, "max"), nc.vector.tensor_scalar(r, r, -SIN_MAX, None, ALU.max))

                def short_conv():
                    for m in range(2):
                        cb, cc, ch = (QK2[:, 13 + 2 * i + m, :] for i in range(3))
                        for i in range(3):
                            dve.wait_ge(*at("raw_copied", (("mix_in", l), 8 + 2 * i + m)))
                        own("cv_step", (l, m, "u"), nc.vector.tensor_tensor(cc, cc, ch, ALU.mult))
                        own("cv_step", (l, m, 2), nc.vector.tensor_scalar(ch, cc, prm("conv_w_2", l * 6 + 4 + m), None,
                                                                         ALU.mult))
                        for back, tap in ((1, 1), (2, 0)):
                            own("cv_step", (l, m, tap), nc.vector.scalar_tensor_tensor(
                                ch[:, back:SEQ], cc[:, 0:SEQ - back], prm("conv_w_2", l * 6 + 2 * tap + m), ch[:, back:SEQ],
                                ALU.mult, ALU.add))
                        own("cv_step", (l, m, "y"), nc.vector.tensor_tensor(ch, ch, cb, ALU.mult))

                def beside(step):
                    if step == 2 and l == 0:
                        angles((0, 1))
                    if step == INDEX_FIRST:
                        dve.wait_ge(*at("v_copied", (("mix_in", l), 3)))
                        own("idx_step", (l, "weights"), nc.vector.tensor_scalar(IW[:, :, :], DV[:, :, 64:72], 8.0 ** -0.5,
                                                                               None, ALU.mult))
                    for n in index_logits(step):
                        t, h = INDEX_STEPS[n]
                        nk = (t + 1) * P
                        sc = DMASK[:, t, 0:nk]
                        w = IW[:, t, h:h + 1]
                        dve.wait_ge(*at("idx_relu", (l, n)))
                        if h == 0:
                            ins = nc.vector.tensor_scalar(sc, TMP[n % 2][:, 0:nk], w, None, ALU.mult)
                        else:
                            ins = nc.vector.scalar_tensor_tensor(sc, TMP[n % 2][:, 0:nk], w, sc, ALU.mult, ALU.add)
                        own("idx_step", (l, n), ins)
                        if h == 7:
                            last = DMASK[:, t, t * P:nk]
                            own("idx_step", (l, t, "causal"), nc.vector.tensor_tensor(last, last, CAUSAL, ALU.add))
                    if index_rounds(step) is not None:
                        t, r0, nr = index_rounds(step)
                        sc = DMASK[:, t, 0:(t + 1) * P]
                        for r in range(r0, r0 + nr):
                            own("idx_step", (l, t, r, "max"), nc.vector.max(TOP8[:, :], sc))
                            own("idx_step", (l, t, r, "out"), nc.vector.match_replace(sc, TOP8[:, :], sc, TAKEN))
                        if r == TOPK // 8 - 1:
                            own("idx_step", (l, t, "mask"), nc.vector.tensor_scalar(sc, sc, TAKEN / 2, NEG, ALU.is_gt,
                                                                                   ALU.mult))
                    if step == CONV_STEP:
                        short_conv()
                    if step == CONV_STEP + 2:
                        dve.wait_ge(*at("bias2_in", (l, 5)))
                        for h in range(6):
                            nc.vector.tensor_tensor(TBK[:, h, P:2 * P], TBK[:, h, P:2 * P], CAUSAL, ALU.add).then_inc(
                                *mark("bias_step", ("causal", l, h)))
                        nc.vector.tensor_copy(DMASK[:, 0, 0:P], CAUSAL).then_inc(*mark("bias_step", ("first", l)))

                if l == 0:
                    dve.wait_ge(*at("tab_in", ("pos", l)))
                    own("trig_step", (l, "float"), nc.vector.tensor_copy(TMP[0], POSI[:, :]))
                    angles((2, 3))
                project(("mix_in", l), mixer_tiles(), FIRST["mix_in", l], SEQ, QK2, 0, ROPE2,
                        lambda t: DV[:, :, :] if t["kind"] == "dv" else VN2[:, :, t["col"]:t["col"] + P], beside)
                stage_end()
                for m in range(2):
                    dve.wait_ge(*at("cv_hi", (l, m)))
                    lo("cv_step", (l, m, "lo"), HL[:, m, :], QK2[:, 17 + m, :], HH[:, m, :])
                attend(number_attention(("att2", l), attention_units_2(l)))
                stage_end()
                dve.wait_ge(*at("mem_hi_made", l))
                lo("mem_lo_made", l, ML[:, :, :], CT[:, :, :], MH[:, :, :])
                out_proj(("mix_out", l), FIRST["mix_out", l], SEQ, XT, lambda k: None, ("ln1", l))
                stage_end()
                layer_norm(("ln1", l))
                for n in range(KT, 2 * KT):
                    dve.wait_ge(*at("v_turned", (("mem_kv", l), n)))
                    nc.vector.tensor_copy(MV[:, :, (n - KT) * P:(n - KT + 1) * P],
                                          PS[:, 4 + n % 2, 0:MEM].rearrange("p (t c) -> p t c", c=P)).then_inc(
                                              *mark("v_copied", (("mem_kv", l), n)))
                stage_end()
                attend(number_attention(("att3", l), attention_units_3()))
                stage_end()
                out_proj(("mem_out", l), FIRST["mem_out", l], SEQ, XT, lambda k: None, ("ln2", l))
                stage_end()
                layer_norm(("ln2", l))
                ffn(("ff", l), FIRST["ff", l], SEQ, l, GROUPS_2, 1, XT, lambda k: None, ("ln3", l))
                stage_end()
                layer_norm(("ln3", l))


_INS = ['x', 'c', 'ctx', 'c_ctx', 'w_ada', 'b_ada', 'g_norm1', 'w_in', 'gq_a', 'gk_a', 'gq_b', 'gk_b', 'rpb_b', 'gq_c',
        'gk_c', 'lambda_q1', 'lambda_k1', 'lambda_q2', 'lambda_k2', 'g_subln', 'w_out', 'g_norm2', 'w_up', 'conv_w',
        'conv_b', 'w_down', 'mem_2', 'positions_2', 'w_in_2', 'conv_w_2', 'rel_bias_2', 'w_mix_out_2', 'ln1_g_2',
        'ln1_b_2', 'w_mq_2', 'w_mkv_2', 'w_mo_2', 'ln2_g_2', 'ln2_b_2', 'w_ff1_2', 'w_ff2_2', 'ln3_g_2', 'ln3_b_2']


def kernel(**inputs):
    import numpy as _np
    import concourse.bacc as _bacc
    from concourse import mybir as _mybir
    from concourse.bass_utils import run_bass_kernel_spmd as _run

    arrays = {name: _np.ascontiguousarray(inputs[name]) for name in _INS if name != "rel_bias_2"}
    arrays["rel_reversed"] = _np.ascontiguousarray(_np.asarray(inputs["rel_bias_2"])[:, :, ::-1])
    arrays.update(constant_arrays())

    def program(counts):
        nc = _bacc.Bacc("TRN2", target_bir_lowering=False, num_devices=1)
        aps = {name: nc.dram_tensor(f"in_{name}_dram", a.shape, _mybir.dt.from_np(a.dtype), kind="ExternalInput").ap()
               for name, a in arrays.items()}
        out = nc.dram_tensor("out_0_dram", (1, SEQ, D), F32, kind="ExternalOutput").ap()
        build(nc, aps, out, counts)
        return nc

    counts = {}
    program(counts)
    nc = program(counts)
    r = _run(nc, [{f"in_{name}_dram": a for name, a in arrays.items()}], core_ids=[0])
    return r.results[0]["out_0_dram"]
```
